# Optimizing a Trainium2 kernel written in Bass

```python
import math
import jax, jax.numpy as jnp
from jax import lax
import numpy as np

D_MODEL = 1024
BATCH = 1
SEQ = 256
DEPTH = 2

CHUNK = 64
N_A_LAYERS = DEPTH // 2
N_B_LAYERS = DEPTH - N_A_LAYERS
N_DENSE_LAYERS = (DEPTH + 1) // 2
N_MOE_LAYERS = DEPTH // 2
A_QK_DIM = 64
A_V_DIM = 2 * A_QK_DIM
A_HEADS = D_MODEL // (2 * A_QK_DIM)
A_QK_WIDTH = A_HEADS * 2 * A_QK_DIM
A_V_WIDTH = A_HEADS * A_V_DIM
B_HEAD_DIM = 64
B_Q_HEADS = D_MODEL // B_HEAD_DIM
B_KV_HEADS = 4
B_GROUP = B_Q_HEADS // B_KV_HEADS
WINDOW = 128
WINDOW_CHUNKS = WINDOW // CHUNK
BAND = WINDOW_CHUNKS * CHUNK
N_BUCKETS = 32
MAX_DISTANCE = 128
N_BIAS_HEADS = B_Q_HEADS
D_FF = 2816
N_EXPERTS = 8
TOP_K = 2
D_EXPERT = 3584
Q_BLOCK = 128
MOE_BLOCK = 256
ADA_SCALE = 0.5
EPS = 1e-6
NEG_INF = -1e30

kernel_name = "yoco_diffattn_swa_sink_moe_encoder"

def rms_norm(x, g):
    xf = x.astype(jnp.float32)
    y = xf * lax.rsqrt(jnp.mean(xf * xf, axis=-1, keepdims=True) + EPS)
    return (y * g.astype(jnp.float32)).astype(x.dtype)

def modulate(h, shift, scale):
    return h * (1 + scale[:, None, :]) + shift[:, None, :]

def t5_bucket(rel):
    nb = N_BUCKETS // 2
    ret = (rel > 0).astype(np.int32) * nb
    n = np.abs(rel)
    max_exact = nb // 2
    large = max_exact + (np.log(np.maximum(n, 1) / max_exact) / np.log(MAX_DISTANCE / max_exact)
                         * (nb - max_exact)).astype(np.int32)
    large = np.minimum(large, nb - 1)
    return (ret + np.where(n < max_exact, n, large)).astype(np.int32)

def swiglu(h, w_in, w_out):
    g, u = jnp.split(h @ w_in, 2, axis=-1)
    return (jax.nn.silu(g) * u) @ w_out

def diff_attention(h, w_qkv, q_gain, k_gain, lam_vec, subln_gain, w_o, rel_bias, lam_init):
    B, S, _ = h.shape
    qkv = h @ w_qkv
    q = qkv[..., :A_QK_WIDTH].reshape(B, S, A_HEADS, 2, A_QK_DIM)
    k = qkv[..., A_QK_WIDTH:2 * A_QK_WIDTH].reshape(B, S, A_HEADS, 2, A_QK_DIM)
    v = qkv[..., 2 * A_QK_WIDTH:].reshape(B, S, A_HEADS, A_V_DIM)
    q = rms_norm(q, q_gain) * (A_QK_DIM ** -0.5)
    k = rms_norm(k, k_gain)
    lam = (jnp.exp(jnp.sum(lam_vec[0] * lam_vec[1]).astype(jnp.float32))
           - jnp.exp(jnp.sum(lam_vec[2] * lam_vec[3]).astype(jnp.float32)) + lam_init)
    outs = []
    for i in range(S // Q_BLOCK):
        q0, L = i * Q_BLOCK, (i + 1) * Q_BLOCK
        qpos = np.arange(q0, L)
        kpos = np.arange(L)
        mask = jnp.asarray((kpos[None, :] // CHUNK) <= (qpos[:, None] // CHUNK))
        bias = jnp.take(rel_bias, jnp.asarray(t5_bucket(kpos[None, :] - qpos[:, None])), axis=0)
        bias = bias.reshape(Q_BLOCK, L, A_HEADS, 2).transpose(3, 2, 0, 1).astype(jnp.float32)
        logits = jnp.einsum('bqhmd,bkhmd->mbhqk', q[:, q0:L], k[:, :L]).astype(jnp.float32)
        logits = jnp.where(mask, logits + bias[:, None], NEG_INF)
        p = jax.nn.softmax(logits, axis=-1)
        attn = p[0] - lam * p[1]
        outs.append(jnp.einsum('bhqk,bkhe->bqhe', attn.astype(v.dtype), v[:, :L]))
    o = jnp.concatenate(outs, axis=1)
    o = rms_norm(o, subln_gain) * (1.0 - lam_init)
    return o.reshape(B, S, A_V_WIDTH) @ w_o

def shared_window_kv(x, cond, ada_w, ada_b, norm_g, w_kv, k_gain):
    B, S, _ = x.shape
    nC = S // CHUNK
    shift, scale = jnp.split(cond @ ada_w + ada_b, 2, axis=-1)
    h = modulate(rms_norm(x, norm_g), shift, scale)
    k, v = jnp.split(h @ w_kv, 2, axis=-1)
    k = rms_norm(k.reshape(B, nC, CHUNK, B_KV_HEADS, B_HEAD_DIM), k_gain)
    v = v.reshape(B, nC, CHUNK, B_KV_HEADS, B_HEAD_DIM)

    def band(t):
        tp = jnp.concatenate([jnp.zeros_like(t[:, :WINDOW_CHUNKS - 1]), t], axis=1)
        return jnp.concatenate([tp[:, i:i + nC] for i in range(WINDOW_CHUNKS)], axis=2)

    return band(k), band(v)

def window_attention(h, w_q, q_gain, sinks, w_o, k_band, v_band, band_bias, band_mask):
    B, S, _ = h.shape
    nC = S // CHUNK
    q = (h @ w_q).reshape(B, nC, CHUNK, B_KV_HEADS, B_GROUP, B_HEAD_DIM)
    q = rms_norm(q, q_gain) * (B_HEAD_DIM ** -0.5)
    logits = jnp.einsum('bcqhgd,bcjhd->bchgqj', q, k_band).astype(jnp.float32) + band_bias
    logits = jnp.where(band_mask[None, :, None, None, None, :], logits, NEG_INF)
    sink = sinks.astype(jnp.float32).reshape(B_KV_HEADS, B_GROUP, 1, 1)
    m = jnp.maximum(jnp.max(logits, axis=-1, keepdims=True), sink)
    p = jnp.exp(logits - m)
    p = p / (jnp.sum(p, axis=-1, keepdims=True) + jnp.exp(sink - m))
    o = jnp.einsum('bchgqj,bcjhe->bcqhge', p.astype(v_band.dtype), v_band)
    return o.reshape(B, S, B_Q_HEADS * B_HEAD_DIM) @ w_o

def moe_swiglu(h, w_router, b_router, w_in, w_out):
    B, S, D = h.shape
    t = h.reshape(-1, D)
    N = t.shape[0]
    M = N * TOP_K
    logits = (t @ w_router + b_router).astype(jnp.float32)
    top_val, top_idx = lax.top_k(logits, TOP_K)
    wts = jax.nn.softmax(top_val, axis=-1).astype(t.dtype)
    flat_e = top_idx.reshape(-1).astype(jnp.int32)
    flat_tok = jnp.repeat(jnp.arange(N, dtype=jnp.int32), TOP_K)
    flat_w = wts.reshape(-1)
    order = jnp.argsort(flat_e)
    e_sorted = flat_e[order]
    counts = jnp.bincount(flat_e, length=N_EXPERTS)
    padded = ((counts + MOE_BLOCK - 1) // MOE_BLOCK) * MOE_BLOCK
    pad_end = jnp.cumsum(padded)
    pad_start = pad_end - padded
    start = jnp.cumsum(counts) - counts
    dest = pad_start[e_sorted] + jnp.arange(M, dtype=jnp.int32) - start[e_sorted]
    n_blocks = (M + N_EXPERTS * (MOE_BLOCK - 1) + MOE_BLOCK - 1) // MOE_BLOCK
    P = n_blocks * MOE_BLOCK
    buf_tok = jnp.zeros((P,), jnp.int32).at[dest].set(flat_tok[order])
    buf_w = jnp.zeros((P,), t.dtype).at[dest].set(flat_w[order])
    block_start = jnp.arange(n_blocks, dtype=jnp.int32) * MOE_BLOCK
    block_expert = jnp.minimum(jnp.sum(pad_end[None, :] <= block_start[:, None], axis=1),
                               N_EXPERTS - 1)
    x_blocks = t[buf_tok].reshape(n_blocks, MOE_BLOCK, D)

    def expert_block(args):
        xb, e = args
        return swiglu(xb, w_in[e], w_out[e])

    y = lax.map(expert_block, (x_blocks, block_expert)).reshape(P, D)
    out = jnp.zeros_like(t).at[buf_tok].add(y * buf_w[:, None])
    return out.reshape(B, S, D)

def setup_inputs(seed: int = 0) -> dict:
    key = jax.random.key(seed)
    ks = iter(jax.random.split(key, 40))
    D = D_MODEL

    def w(shape, fan_in, scale=1.0):
        return jax.random.normal(next(ks), shape, jnp.float32) * (scale * fan_in ** -0.5)

    def gain(shape):
        return 1.0 + 0.05 * jax.random.normal(next(ks), shape, jnp.float32)

    def small(shape, s):
        return s * jax.random.normal(next(ks), shape, jnp.float32)

    return {
        "x": jax.random.normal(next(ks), (BATCH, SEQ, D), jnp.float32),
        "c": jax.random.normal(next(ks), (BATCH, D), jnp.float32),
        "ada_w": w((DEPTH, D, 6 * D), D, ADA_SCALE),
        "ada_b": small((DEPTH, 6 * D), 0.02),
        "norm_attn": gain((DEPTH, D)),
        "norm_ffn": gain((DEPTH, D)),
        "rel_bias": small((N_BUCKETS, N_BIAS_HEADS), 0.5),
        "a_w_qkv": w((N_A_LAYERS, D, 2 * A_QK_WIDTH + A_V_WIDTH), D),
        "a_q_norm": gain((N_A_LAYERS, A_QK_DIM)),
        "a_k_norm": gain((N_A_LAYERS, A_QK_DIM)),
        "a_lambda": small((N_A_LAYERS, 4, A_QK_DIM), 0.1),
        "a_subln": gain((N_A_LAYERS, A_V_DIM)),
        "a_w_o": w((N_A_LAYERS, A_V_WIDTH, D), A_V_WIDTH),
        "kv_ada_w": w((D, 2 * D), D, ADA_SCALE),
        "kv_ada_b": small((2 * D,), 0.02),
        "kv_norm": gain((D,)),
        "kv_w": w((D, 2 * B_KV_HEADS * B_HEAD_DIM), D),
        "kv_k_norm": gain((B_HEAD_DIM,)),
        "b_w_q": w((N_B_LAYERS, D, B_Q_HEADS * B_HEAD_DIM), D),
        "b_q_norm": gain((N_B_LAYERS, B_HEAD_DIM)),
        "b_sinks": small((N_B_LAYERS, B_Q_HEADS), 0.5),
        "b_w_o": w((N_B_LAYERS, B_Q_HEADS * B_HEAD_DIM, D), B_Q_HEADS * B_HEAD_DIM),
        "ffn_w_in": w((N_DENSE_LAYERS, D, 2 * D_FF), D),
        "ffn_w_out": w((N_DENSE_LAYERS, D_FF, D), D_FF),
        "moe_router_w": w((N_MOE_LAYERS, D, N_EXPERTS), D),
        "moe_router_b": small((N_MOE_LAYERS, N_EXPERTS), 0.01),
        "moe_w_in": w((N_MOE_LAYERS, N_EXPERTS, D, 2 * D_EXPERT), D),
        "moe_w_out": w((N_MOE_LAYERS, N_EXPERTS, D_EXPERT, D), D_EXPERT),
    }

def reference(x, c, ada_w, ada_b, norm_attn, norm_ffn, rel_bias,
              a_w_qkv, a_q_norm, a_k_norm, a_lambda, a_subln, a_w_o,
              kv_ada_w, kv_ada_b, kv_norm, kv_w, kv_k_norm,
              b_w_q, b_q_norm, b_sinks, b_w_o,
              ffn_w_in, ffn_w_out,
              moe_router_w, moe_router_b, moe_w_in, moe_w_out):
    S = x.shape[1]
    nC = S // CHUNK
    cond = jax.nn.silu(c)
    qo = np.arange(CHUNK)
    jo = np.arange(BAND)
    band_rel = jo[None, :] - (WINDOW_CHUNKS - 1) * CHUNK - qo[:, None]
    band_bias = jnp.take(rel_bias, jnp.asarray(t5_bucket(band_rel)), axis=0)
    band_bias = band_bias.transpose(2, 0, 1).reshape(B_KV_HEADS, B_GROUP, CHUNK, BAND)
    band_bias = band_bias.astype(jnp.float32)
    band_mask = jnp.asarray((np.arange(nC)[:, None] - (WINDOW_CHUNKS - 1)
                             + (jo // CHUNK)[None, :]) >= 0)
    k_band = v_band = None
    for l in range(DEPTH):
        mod = cond @ ada_w[l] + ada_b[l]
        sh_a, sc_a, g_a, sh_f, sc_f, g_f = jnp.split(mod, 6, axis=-1)
        h = modulate(rms_norm(x, norm_attn[l]), sh_a, sc_a)
        if l < N_A_LAYERS:
            y = diff_attention(h, a_w_qkv[l], a_q_norm[l], a_k_norm[l], a_lambda[l], a_subln[l],
                               a_w_o[l], rel_bias, 0.8 - 0.6 * math.exp(-0.3 * l))
        else:
            j = l - N_A_LAYERS
            y = window_attention(h, b_w_q[j], b_q_norm[j], b_sinks[j], b_w_o[j],
                                 k_band, v_band, band_bias, band_mask)
        x = x + g_a[:, None, :] * y
        h = modulate(rms_norm(x, norm_ffn[l]), sh_f, sc_f)
        if l % 2 == 0:
            y = swiglu(h, ffn_w_in[l // 2], ffn_w_out[l // 2])
        else:
            y = moe_swiglu(h, moe_router_w[l // 2], moe_router_b[l // 2],
                           moe_w_in[l // 2], moe_w_out[l // 2])
        x = x + g_f[:, None, :] * y
        if l == N_A_LAYERS - 1:
            k_band, v_band = shared_window_kv(x, cond, kv_ada_w, kv_ada_b, kv_norm, kv_w,
                                              kv_k_norm)
    return x


_drawn_inputs = setup_inputs


def setup_inputs(seed=0):
    import zlib

    import numpy as np

    out = dict(_drawn_inputs(seed))
    spreads = {}
    factors = {'norm_attn': 3.619,
     'a_q_norm': 5.012,
     'a_k_norm': 6.124,
     'a_subln': 2.823,
     'kv_ada_b': 4.77,
     'kv_norm': 3.817,
     'kv_k_norm': 7.118,
     'b_q_norm': 8.0,
     'b_sinks': 8.0,
     'moe_router_b': 13.69}
    for name, (base, spread) in spreads.items():
        noise = np.random.default_rng([zlib.crc32(name.encode()), seed]).standard_normal(out[name].shape)
        drawn = base * np.exp(spread * noise) if base else spread * noise
        out[name] = __import__('jax').numpy.asarray(drawn.astype(out[name].dtype))
    for name, factor in factors.items():
        out[name] = (out[name] * factor).astype(out[name].dtype)
    return out
```

```python
import math
from contextlib import ExitStack

import concourse.bass as bass
import numpy as np
from concourse import mybir

ALU = mybir.AluOpType
ACT = mybir.ActivationFunctionType
AX = mybir.AxisListType.X
F32 = mybir.dt.float32
F32R = mybir.dt.float32r
I32 = mybir.dt.int32

P = 128
D = 1024
KT = D // P
TB = 2
UNIT = 1024
RAW_SLOTS = 12
SPLIT_SLOTS = 6
ADA_SLOTS = 4
HEADS = 8
NBIAS = 16
D_FF = 2816
FC = 256
FF_STEPS = D_FF // FC
N_EXP = 8
D_EXP = 3584
EC = 512
E_STEPS = D_EXP // EC
EPS = 1e-6
NEG = -1e30
LAM_INIT = 0.8 - 0.6 * math.exp(-0.3 * 0)
SPAN = 3 * P

TOEP_SLOTS = 2 * (TB * D // SPAN)

U_QKV = 0
U_WO = U_QKV + 3 * KT
U_FF = U_WO + KT
FF_IN = KT // 2
FF_OUT = FC // P
U_KV = U_FF + FF_STEPS * (FF_IN + FF_OUT)
U_BQ = U_KV + KT // 2
U_BO = U_BQ + KT
U_MOE = U_BO + KT
E_IN = KT
E_OUT = EC // P
E_UNITS = E_IN + E_OUT
MOE_STEPS = N_EXP * E_STEPS
U_END = U_MOE + MOE_STEPS * E_UNITS

MOD0 = (0, 1, 2, 3, 4, 6)
MOD1 = (0, 1, 2, 3, 4, 5)
MODKV = (7, 8)

CST_IDENT, CST_TRI, CST_IOTA, CST_ONES, CST_LOWER = 0, 128, 256, 384, 512
CST_COLS = 512 + N_EXP * N_EXP


class Units:

    def __init__(self, first, turn=0, per_turn=0):
        assert per_turn % RAW_SLOTS == 0
        self.first, self.turn, self.per = first, turn, per_turn

    def raw(self, k):
        return (self.first + k) % RAW_SLOTS

    def split(self, k):
        return (self.first + k) % SPLIT_SLOTS

    def count(self, k):
        return self.turn * self.per + (self.first + k) if self.per else self.first + k

    def landed(self, k):
        n = 16 * ((self.first + k) // RAW_SLOTS + 1)
        return self.turn * (16 * self.per // RAW_SLOTS) + n if self.per else n


class Chain:

    def __init__(self, engine, sem):
        self.engine, self.sem, self.n, self.base = engine, sem, 0, None

    def __call__(self, instruction):
        instruction.then_inc(self.sem, 1)
        self.n += 1
        self.engine.wait_ge(self.sem, self.n if self.base is None else self.base + self.n)


def chunk_dynamic(turn):
    return not isinstance(turn, int)


def trunk(nc, t):
    ctx = ExitStack()
    with ctx:
        def sb(name, shape, dtype=F32):
            return ctx.enter_context(nc.sbuf_tensor(name, shape, dtype))

        def sem(name):
            return ctx.enter_context(nc.semaphore(name))

        WRAW = sb("WRAW", [P, RAW_SLOTS, UNIT])
        WHI = sb("WHI", [P, SPLIT_SLOTS, UNIT], F32R)
        WLO = sb("WLO", [P, SPLIT_SLOTS, UNIT], F32R)
        MOD = sb("MOD", [P, 9, D])
        SHR = sb("SHR", [P, 4 * D])
        X = sb("X", [P, TB, D])
        H = sb("H", [P, TB, D])
        HT_HI = sb("HT_HI", [P, KT, TB * P], F32R)
        HT_LO = sb("HT_LO", [P, KT, TB * P], F32R)
        Q = sb("Q", [P, TB, D])
        AT_HI = sb("AT_HI", [P, 512], F32R)
        AT_LO = sb("AT_LO", [P, 512], F32R)
        W4 = sb("W4", [P, D])
        S = sb("S", [P, 2, 2, 256])
        CST = sb("CST", [P, CST_COLS])
        condT = sb("condT", [P, KT])
        gcol = sb("gcol", [P, 8])
        lamv = W4[:, 0:256]
        relb = sb("relb", [32, NBIAS])
        sinks = sb("sinks", [P, NBIAS])
        wr = sb("wr", [P, KT * N_EXP])
        wr_hi = sb("wr_hi", [P, KT * N_EXP], F32R)
        wr_lo = sb("wr_lo", [P, KT * N_EXP], F32R)
        rb = sb("rb", [P, N_EXP])
        ss = sb("ss", [P, TB, 16])
        nx = sb("nx", [P, TB, 2])
        sm = sb("sm", [P, 2, 16])
        neglam = sb("neglam", [P, 4])
        rt = sb("rt", [P, 8, TB * N_EXP])
        flag = sb("flag", [1, 1], I32)
        PS = ctx.enter_context(nc.psum_tensor("PS", [P, 8, 512], F32))
        TOEP = nc.dram_tensor("toep_rows", (NBIAS, P, SPAN), F32)

        ident = CST[:, CST_IDENT:CST_IDENT + P]
        tri = CST[:, CST_TRI:CST_TRI + P]
        iota = CST[:, CST_IOTA:CST_IOTA + P]
        ones = CST[:, CST_ONES:CST_ONES + P]
        ADA = SHR[:, :].rearrange("p (s n) -> p s n", s=ADA_SLOTS)
        BIAS = SHR[:, :].rearrange("p (h k) -> p h k", h=NBIAS)
        ACC = H
        GB = S[:, :, :, :].rearrange("p a b k -> p (a b k)")
        K = MOD[:, 7:9, :]
        V = H
        onehot = W4[0:32, 512:512 + SPAN]
        PT = W4[:, :].rearrange("p (n m k) -> p n m k", n=2, m=2)

        def toep_rows(h):
            j = h % TOEP_SLOTS
            place = (Q if j < TOEP_SLOTS // 2 else K)[:, :, :].rearrange("p i n -> p (i n)")
            j %= TOEP_SLOTS // 2
            return place[:, j * SPAN:(j + 1) * SPAN]

        FSIL = Q[:, 0, 0:512].rearrange("p (i f) -> p i f", i=TB)
        FACT = Q[:, 0, 512:1024].rearrange("p (i f) -> p i f", i=TB)
        KBT = MOD[:, 7, :].rearrange("p (j k) -> p j k", j=4)
        KV = MOD[:, 8, :].rearrange("p (i n) -> p i n", i=TB)
        KDUP = MOD[:, 6, :].rearrange("p (i j c d) -> p i j c d", i=TB, j=4, c=2)
        SEL = SHR[:, 0:2048].rearrange("p (e i s) -> p e i s", e=N_EXP, i=TB)
        SELT = SHR[:, 2048:4096].rearrange("p (e t) -> p e t", e=N_EXP)
        XACC = MOD[:, 0:2, :]
        Y = MOD[:, 2, :]
        EACT = MOD[:, 3, 0:512]
        ESIL = MOD[:, 4, 0:512]
        SELT_CUR = MOD[:, 6, 0:256]
        OUT = MOD[:, 7:9, :]
        SELW = GB.rearrange("p (e i s) -> p e i s", e=4, i=TB)
        XT_HI = HT_HI[:, 0:4, :].rearrange("p a (b s) -> p (a b) s", b=2)
        XT_LO = HT_LO[:, 0:4, :].rearrange("p a (b s) -> p (a b) s", b=2)

        def f32(ap):
            return ap.bitcast(F32)

        w_landed = [sem(f"w_landed{r}") for r in range(RAW_SLOTS)]
        w_landed_b = [sem(f"w_landed_b{r}") for r in range(RAW_SLOTS)]
        w_hi = sem("w_hi")
        w_lo = sem("w_lo")
        w_used = sem("w_used")
        ada_landed = [sem(f"ada_landed{r}") for r in range(ADA_SLOTS)]
        ada_used = sem("ada_used")
        mod_sum = sem("mod_sum")
        mod_ready = sem("mod_ready")
        x_landed = sem("x_landed")
        cst_landed = sem("cst_landed")
        small_landed = sem("small_landed")
        modb_landed = sem("modb_landed")
        gain_landed = sem("gain_landed")
        toep_mm = sem("toep_mm")
        toep_sbuf = sem("toep_sbuf")
        toep_dram = [sem(f"toep_dram{j}") for j in range(TOEP_SLOTS)]
        bias_landed = sem("bias_landed")
        cond_ready = sem("cond_ready")
        gain_used = sem("gain_used")
        sq_ready = sem("sq_ready")
        var_ready = sem("var_ready")
        root_ready = sem("root_ready")
        sq_read = sem("sq_read")
        h_ready = sem("h_ready")
        ht_psum = sem("ht_psum")
        ht_hi = sem("ht_hi")
        ht_lo = sem("ht_lo")
        qk_norm = sem("qk_norm")
        v_copied = sem("v_copied")
        qkt_psum = sem("qkt_psum")
        qkt_ready = sem("qkt_ready")
        bias_masked = sem("bias_masked")
        attn = {}
        for a in "AB":
            attn[a] = {n: sem(f"{n}_{a}") for n in (
                "logits", "biased", "negmax", "expd", "probs", "pt_psum", "pt_ready", "pv", "o_ready")}
        x_new = sem("x_new")
        silu_ready = sem("silu_ready")
        act_ready = sem("act_ready")
        at_psum = sem("at_psum")
        at_hi = sem("at_hi")
        at_ready = sem("at_ready")
        kv_ready = sem("kv_ready")
        kdup_ready = sem("kdup_ready")
        kbt_psum = sem("kbt_psum")
        kbt_ready = sem("kbt_ready")
        wr_hi_ready = sem("wr_hi_ready")
        wr_ready = sem("wr_ready")
        r_logits = sem("r_logits")
        r_shift = sem("r_shift")
        r_exp = sem("r_exp")
        mask_ready = sem("mask_ready")
        pos_psum = sem("pos_psum")
        flag_ready = sem("flag_ready")
        selw_ready = sem("selw_ready")
        selt_psum = sem("selt_psum")
        selt_ready = sem("selt_ready")
        sel_ready = sem("sel_ready")
        g_psum = sem("g_psum")
        xt_hi = sem("xt_hi")
        xt_ready = sem("xt_ready")
        e_silu, e_act = sem("e_silu"), sem("e_act")
        e_at_psum, e_at_hi, e_at = sem("e_at_psum"), sem("e_at_hi"), sem("e_at")
        ey_ready = sem("ey_ready")
        selt_cur = sem("selt_cur")
        sc_psum = sem("sc_psum")
        sc_added = sem("sc_added")
        out_ready, out_stored = sem("out_ready"), sem("out_stored")
        dve_chain = sem("dve_chain")
        x_squares = sem("x_squares")

        x_v = t["x"].rearrange("b (i p) d -> p (b i) d", p=P)
        out_v = t["out"].rearrange("b (i p) d -> p (b i) d", p=P)
        ffin_v = t["ffn_w_in"].rearrange("l (u k p) (c f) -> (l u) p k c f", k=2, p=P, c=2)
        ein_v = t["moe_w_in"].rearrange("l e (k p) (c j f) -> (l e) j k p c f", p=P, c=2, j=E_STEPS)
        eout_v = t["moe_w_out"].rearrange("l e (s p) d -> (l e s) p d", p=P)
        kvw_v = t["kv_w"].rearrange("(u k p) n -> u p k n", k=2, p=P)
        SMALL = 16

        def overflow(engine):
            engine.wait_ge(flag_ready, 1)
            over = engine.value_load(flag[0:1, 0:1], min_val=0, max_val=1)
            return engine.If(over > 0)

        block = ctx.enter_context(nc.Block())

        @block.sync
        def _(sp):
            sp.dma_start(X[:, :, :], x_v).then_inc(x_landed, 16)
            sp.dma_start(CST[:, :], t["cst"]).then_inc(cst_landed, 16)

            def load(u, k, src, first_round=False, dst_shape=None):
                if not first_round:
                    sp.wait_ge(w_lo, u.count(k - RAW_SLOTS) + 1)
                dst = WRAW[:, u.raw(k), :]
                if dst_shape is not None:
                    dst = dst.rearrange(*dst_shape[0], **dst_shape[1])
                sp.dma_start(dst, src).then_inc(w_landed[u.raw(k)], 16)

            u = Units(U_QKV)
            for g in range(3):
                for k in range(KT):
                    n = g * KT + k
                    load(u, n, t["a_w_qkv"][0, k * P:(k + 1) * P, g * D:(g + 1) * D], n < RAW_SLOTS)
            u = Units(U_WO)
            for k in range(KT):
                load(u, k, t["a_w_o"][0, k * P:(k + 1) * P, :])

            def ff_load_in(u, k0, s):
                for k in range(FF_IN):
                    sp.wait_ge(w_lo, u.count(k0 + k - RAW_SLOTS) + 1)
                    r = u.raw(k0 + k)
                    for kt, landed in enumerate((w_landed[r], w_landed_b[r])):
                        sp.dma_start(WRAW[:, r, kt * 512:kt * 512 + 512].rearrange("p (c f) -> p c f", c=2),
                                     ffin_v[k][:, kt, :, bass.ds(s * FC, FC)]).then_inc(landed, 16)

            def ff_load_out(u, k0, s):
                for k in range(FF_OUT):
                    load(u, k0 + k, t["ffn_w_out"][0, bass.ds(s * FC + k * P, P), :])

            ff_load_in(Units(U_FF), 0, 0)
            first = U_FF + FF_IN
            with sp.Fori(0, (FF_STEPS - 1) // 2) as it:
                u = Units(first, it, RAW_SLOTS)
                for b in range(2):
                    ff_load_in(u, 6 * b, it * 2 + (b + 1))
                    ff_load_out(u, 6 * b + FF_IN, it * 2 + b)
            ff_load_out(Units(U_KV - FF_OUT), 0, FF_STEPS - 1)

            u = Units(U_KV)
            for k in range(KT // 2):
                load(u, k, kvw_v[k], dst_shape=(("p (k n) -> p k n",), dict(k=2)))
            for base, w in ((U_BQ, t["b_w_q"]), (U_BO, t["b_w_o"])):
                u = Units(base)
                for k in range(KT):
                    load(u, k, w[0, k * P:(k + 1) * P, :])

            def e_load_in(u, k0, e, j):
                for k in range(E_IN):
                    load(u, k0 + k, ein_v[e][j][k],
                         dst_shape=(("p (c f) -> p c f",), dict(c=2)))

            def e_load_out(u, k0, s):
                for k in range(E_OUT):
                    load(u, k0 + k, eout_v[s * E_OUT + k])

            def moe_loads(p):
                base = U_MOE + p * MOE_STEPS * E_UNITS
                e_load_in(Units(base), 0, 0, 0)
                base += E_IN
                with sp.Fori(0, N_EXP - 1) as e:
                    with sp.Fori(0, E_STEPS - 1) as j:
                        u = Units(base, e * E_STEPS + j, E_UNITS)
                        e_load_in(u, 0, e, j + 1)
                        e_load_out(u, E_IN, e * E_STEPS + j)
                    u = Units(base, e * E_STEPS + (E_STEPS - 1), E_UNITS)
                    e_load_in(u, 0, e + 1, 0)
                    e_load_out(u, E_IN, e * E_STEPS + (E_STEPS - 1))
                e = N_EXP - 1
                with sp.Fori(0, E_STEPS - 1) as j:
                    u = Units(base, e * E_STEPS + j, E_UNITS)
                    e_load_in(u, 0, e, j + 1)
                    e_load_out(u, E_IN, e * E_STEPS + j)
                e_load_out(Units(base + (MOE_STEPS - 1) * E_UNITS), 0, MOE_STEPS - 1)

            def store(p):
                for b in range(TB):
                    sp.wait_ge(out_ready, TB * p + b + 1)
                    sp.dma_start(out_v[:, b, :], OUT[:, b, :]).then_inc(out_stored, 16)
                sp.wait_ge(out_stored, 32 * (p + 1))

            moe_loads(0)
            store(0)
            with overflow(sp):
                moe_loads(1)
                store(1)
                sp.nop()

        @block.gpsimd
        def _(pool):
            small = [
                (condT[:, :], t["c"].rearrange("b (p k) -> p (b k)", p=P)),
                (gcol[0:64, 0:1], t["a_q_norm"].rearrange("l d -> d l")),
                (gcol[64:128, 0:1], t["a_q_norm"].rearrange("l d -> d l")),
                (gcol[0:64, 1:2], t["a_k_norm"].rearrange("l d -> d l")),
                (gcol[64:128, 1:2], t["a_k_norm"].rearrange("l d -> d l")),
                (gcol[:, 2:3], t["a_subln"].rearrange("l d -> d l")),
                (gcol[0:64, 3:4], t["b_q_norm"].rearrange("l d -> d l")),
                (gcol[64:128, 3:4], t["b_q_norm"].rearrange("l d -> d l")),
                (gcol[0:64, 4:5], t["kv_k_norm"].rearrange("(d o) -> d o", o=1)),
                (gcol[64:128, 4:5], t["kv_k_norm"].rearrange("(d o) -> d o", o=1)),
                (lamv, t["a_lambda"].rearrange("l a d -> l (a d)").partition_broadcast(P)),
                (relb[:, :], t["rel_bias"]),
                (onehot, t["onehot"]),
                (sinks[:, :], t["b_sinks"].partition_broadcast(P)),
                (rb[:, :], t["moe_router_b"].partition_broadcast(P)),
                (wr[:, :].rearrange("p (k e) -> p k e", k=KT),
                 t["moe_router_w"].rearrange("l (k p) e -> p (l k) e", p=P)),
            ]
            assert len(small) == SMALL
            for dst, src in small:
                with nc.allow_non_contiguous_dma(reason="short columns of gains"):
                    pool.dma_start(dst, src).then_inc(small_landed, 16)
            for c, slot in enumerate(MOD0):
                pool.dma_start(MOD[:, slot, :], t["ada_b"][0:1, c * D:(c + 1) * D].partition_broadcast(P)
                               ).then_inc(modb_landed, 16)
            pool.dma_start(GB, t["norm_attn"][0:1, :].partition_broadcast(P)).then_inc(gain_landed, 16)

            for h in range(NBIAS):
                pool.wait_ge(toep_sbuf, h + 1)
                pool.dma_start(TOEP.ap()[h], toep_rows(h)).then_inc(toep_dram[h % TOEP_SLOTS], 16)

            def ada_load(chunk, w, col, first=False, turn=0):
                for k in range(KT):
                    n = chunk * KT + k
                    if not (first and k < ADA_SLOTS):
                        pool.wait_ge(ada_used, turn * KT + (n - ADA_SLOTS + 1) if chunk_dynamic(turn)
                                     else n - ADA_SLOTS + 1)
                    pool.dma_start(ADA[:, k % ADA_SLOTS, :], w.rearrange("(p k) n -> k p n", p=P)[k][:, bass.ds(col, D)]
                                   ).then_inc(ada_landed[k % ADA_SLOTS], 16)

            for c in range(6):
                ada_load(c, t["ada_w"][0], c * D, first=c == 0)

            for j in range(TOEP_SLOTS):
                pool.wait_ge(toep_dram[j], 16 * (NBIAS // TOEP_SLOTS + (j < NBIAS % TOEP_SLOTS)))
            pool.wait_ge(ada_used, 6 * KT)
            bias_src = bass.AP(TOEP, P - 1, [[SPAN - 1, P], [P * SPAN, NBIAS], [1, 2 * P]])
            pool.dma_start(BIAS, bias_src).then_inc(bias_landed, 16)
            pool.wait_ge(bias_landed, 16)
            pool.memset(BIAS[0:64, :, 192:256], NEG).then_inc(bias_masked, 1)

            pool.wait_ge(attn["A"]["pt_psum"], TB * HEADS)
            pool.dma_start(GB, t["norm_ffn"][0:1, :].partition_broadcast(P)).then_inc(gain_landed, 16)

            pool.wait_ge(h_ready, 3 * TB)
            for c, slot in enumerate(MOD1):
                pool.dma_start(MOD[:, slot, :], t["ada_b"][1:2, c * D:(c + 1) * D].partition_broadcast(P)
                               ).then_inc(modb_landed, 16)
            for c, slot in enumerate(MODKV):
                pool.dma_start(MOD[:, slot, :],
                               t["kv_ada_b"].rearrange("(o n) -> o n", o=1)[:, c * D:(c + 1) * D]
                               .partition_broadcast(P)).then_inc(modb_landed, 16)
            pool.dma_start(GB, t["kv_norm"].rearrange("(o n) -> o n", o=1).partition_broadcast(P)
                           ).then_inc(gain_landed, 16)
            with pool.Fori(0, 6) as c:
                ada_load(6, t["ada_w"][1], c * D, turn=c)
            for c in range(2):
                ada_load(12 + c, t["kv_ada_w"], c * D)

            pool.wait_ge(ada_used, 14 * KT)
            pool.dma_start(BIAS, bias_src).then_inc(bias_landed, 16)
            pool.wait_ge(gain_used, 3)
            pool.dma_start(GB, t["norm_attn"][1:2, :].partition_broadcast(P)).then_inc(gain_landed, 16)
            pool.wait_ge(bias_landed, 32)
            pool.memset(BIAS[0:64, :, 192:256], NEG).then_inc(bias_masked, 1)
            pool.memset(BIAS[0:64, :, 0:64], NEG).then_inc(bias_masked, 1)
            pool.memset(BIAS[64:128, :, 0:128], NEG).then_inc(bias_masked, 1)
            pool.wait_ge(attn["B"]["pt_psum"], TB * HEADS)
            pool.dma_start(GB, t["norm_ffn"][1:2, :].partition_broadcast(P)).then_inc(gain_landed, 16)

            def scatter_matrices(p):
                pool.wait_ge(selt_ready, 4 * (p + 1))
                if p:
                    pool.wait_ge(sc_psum, 4 * N_EXP)
                pool.tensor_copy(SELT_CUR, SELT[:, 0, :]).then_inc(selt_cur, 1)
                with pool.Fori(1, N_EXP) as e:
                    pool.wait_ge(sc_psum, e * 4 + 4 * N_EXP * p)
                    pool.tensor_copy(SELT_CUR, SELT[:, e, :]).then_inc(selt_cur, 1)

            scatter_matrices(0)
            with overflow(pool):
                scatter_matrices(1)
                pool.nop()

        @block.scalar
        def _(act):
            chain = Chain(act, x_squares)

            def hi(u, *units):
                for k in units:
                    act.wait_ge(w_landed[u.raw(k)], u.landed(k))
                    if u.first + k >= SPLIT_SLOTS:
                        act.wait_ge(w_used, u.count(k - SPLIT_SLOTS) + 1)
                    nc.scalar.activation(WHI[:, u.split(k), :], WRAW[:, u.raw(k), :], ACT.Copy
                                         ).then_inc(w_hi, 1)

            def hi_ff_in(u, units, turn, s0=False):
                first_step = [Units(U_FF).raw(k) for k in range(FF_IN)]
                for k in units:
                    r = u.raw(k)
                    act.wait_ge(w_landed_b[r], 16 if s0 else turn * 16 + (32 if r in first_step else 16))
                    hi(u, k)

            def squares(src, i):
                chain(nc.scalar.activation(W4[:, :], src, ACT.Square, accum_out=nx[:, i, 0:1]))

            roots = [0]

            def root(ap):
                roots[0] += 1
                act.wait_ge(var_ready, roots[0])
                nc.scalar.activation(ap, ap, ACT.Sqrt).then_inc(root_ready, 1)

            def norm_root():
                for i in range(TB):
                    squares(X[:, i, :], i)
                root(nx[:, :, 1:2])

            def ht_his(use, scale=None):
                for b in range(4):
                    act.wait_ge(ht_psum, 4 * use + b + 1)
                    nc.scalar.activation(
                        HT_HI[:, 2 * b:2 * b + 2, :].rearrange("p k s -> p (k s)"), PS[:, b, :], ACT.Copy,
                        **({} if scale is None else dict(scale=scale))).then_inc(ht_hi, 1)

            def transposed(first, dst_of, col, banks, total):
                for n, bank in enumerate(banks):
                    act.wait_ge(total, first + n + 1)
                    nc.scalar.activation(dst_of(n), PS[:, bank, :], ACT.Copy, scale=gcol[:, col:col + 1]
                                         ).then_inc(qkt_ready if total is qkt_psum else kbt_ready, 1)

            def attention(a):
                sems = attn[a]

                def exps(n):
                    i, span = n // HEADS, (n // HEADS + 1) * P
                    act.wait_ge(sems["negmax"], n + 1)
                    if n >= 2:
                        act.wait_ge(sems["probs"], n - 1)
                    for m in range(2):
                        if a == "B":
                            nc.scalar.activation(sm[:, n % 2, 6 + m:7 + m],
                                                 sinks[:, 2 * (n % HEADS) + m:2 * (n % HEADS) + m + 1], ACT.Exp,
                                                 bias=sm[:, n % 2, 2 + m:3 + m])
                        nc.scalar.activation(S[:, n % 2, m, 0:span], S[:, n % 2, m, 0:span], ACT.Exp,
                                             bias=sm[:, n % 2, 2 + m:3 + m],
                                             accum_out=sm[:, n % 2, 4 + m:5 + m]).then_inc(sems["expd"], 1)

                def copy_pt(n):
                    maps = 1 if a == "A" else 2
                    span = (n // HEADS + 1) * P
                    act.wait_ge(sems["pt_psum"], n + 1)
                    if n >= 2:
                        act.wait_ge(sems["pv"], n - 1)
                    nc.scalar.activation(PT[:, n % 2, 0:maps, 0:span],
                                         PS[:, 4 + n % 2, :].rearrange("p (m k) -> p m k", m=2)[:, 0:maps, 0:span],
                                         ACT.Copy).then_inc(sems["pt_ready"], 1)

                def copy_o(n):
                    i, h = n // HEADS, n % HEADS
                    act.wait_ge(sems["pv"], n + 1)
                    nc.scalar.activation(Q[:, i, h * P:(h + 1) * P], PS[:, 6 + n % 2, 0:P], ACT.Copy
                                         ).then_inc(sems["o_ready"], 1)

                n_all = TB * HEADS
                exps(0)
                exps(1)
                for n in range(n_all):
                    copy_pt(n)
                    if n + 2 < n_all:
                        exps(n + 2)
                    copy_o(n)

            act.wait_ge(small_landed, 16 * SMALL)
            nc.scalar.activation(condT[:, :], condT[:, :], ACT.Silu).then_inc(cond_ready, 1)
            for h in range(NBIAS):
                act.wait_ge(toep_mm, h + 1)
                if h >= TOEP_SLOTS:
                    act.wait_ge(toep_dram[h % TOEP_SLOTS], 16)
                nc.scalar.activation(toep_rows(h), PS[:, 4 + h % 4, 0:SPAN], ACT.Copy).then_inc(toep_sbuf, 1)
            act.wait_ge(x_landed, 16)
            act.wait_ge(sq_read, 1)
            nc.scalar.activation(neglam[:, 0:2], neglam[:, 0:2], ACT.Exp).then_inc(sq_ready, 1)
            norm_root()
            ht_his(0)

            u = Units(U_QKV)

            def block_squares(banks_of, width, count, heads):
                for i in range(TB):
                    act.wait_ge(sq_read, count + i)
                    nc.scalar.activation(W4[:, 0:width], banks_of(i), ACT.Square).then_inc(sq_ready, 1)
                    root(ss[:, i, 0:heads])

            def pair(b):
                return PS[:, b:b + 2, :].rearrange("p b n -> p (b n)")

            hi(u, *range(0, 14))
            act.wait_ge(w_used, U_QKV + KT)
            block_squares(lambda i: pair(4 + 2 * i), D, 1, 16)
            hi(u, *range(14, 20))
            act.wait_ge(w_used, U_QKV + 2 * KT)
            block_squares(lambda i: pair(2 * i), D, 3, 16)
            hi(u, *range(20, 24))
            act.wait_ge(w_used, U_WO)
            for i in range(TB):
                nc.scalar.activation(V[:, i, :], pair(4 + 2 * i), ACT.Copy).then_inc(v_copied, 1)
            hi(u, *range(24, 30))
            transposed(0, lambda n: Q[:, n // 2, (n % 2) * 512:(n % 2) * 512 + 512], 0, range(0, 4), qkt_psum)
            transposed(4, lambda n: K[:, n // 2, (n % 2) * 512:(n % 2) * 512 + 512], 1, range(4, 8), qkt_psum)
            attention("A")
            act.wait_ge(attn["A"]["o_ready"], TB * HEADS)
            block_squares(lambda i: Q[:, i, :], D, 5, 8)
            ht_his(1, scale=gcol[:, 2:3])
            hi(u, *range(30, 32))
            hi_ff_in(u, range(32, 36), 0, True)

            act.wait_ge(x_new, 2)
            norm_root()
            ht_his(2)

            def f_silu(u, k):
                act.wait_ge(w_used, u.count(k) + 1)
                nc.scalar.activation(FSIL, PS[:, 0:2, 0:FC], ACT.Silu).then_inc(silu_ready, 1)

            def f_at(n):
                act.wait_ge(at_psum, n)
                nc.scalar.activation(AT_HI[:, :], PS[:, 2, :], ACT.Copy).then_inc(at_hi, 1)

            f_silu(Units(U_FF), FF_IN - 1)
            first = U_FF + FF_IN
            with act.Fori(0, (FF_STEPS - 1) // 2) as it:
                u = Units(first, it, RAW_SLOTS)
                for b in range(2):
                    hi_ff_in(u, range(6 * b, 6 * b + 4), it)
                    f_at(it * 2 + (b + 1))
                    hi(u, 6 * b + 4, 6 * b + 5)
                    f_silu(u, 6 * b + 3)
            f_at(FF_STEPS)
            u = Units(U_KV - FF_OUT)
            hi(u, *range(0, 6))

            act.wait_ge(x_new, 4)
            norm_root()
            ht_his(3)
            act.wait_ge(w_used, U_BQ)
            for i in range(TB):
                nc.scalar.activation(KV[:, i, 256:512], PS[:, 4 + i, 256:512], ACT.Copy)
            block_squares(lambda i: PS[:, 4 + i, 0:256], 256, 7, 4)
            ht_his(4)
            u = Units(U_BQ)
            hi(u, *range(0, 8))
            transposed(0, lambda n: KBT[:, 2 * n:2 * n + 2, :].rearrange("p j k -> p (j k)"), 4,
                       range(0, 2), kbt_psum)
            act.wait_ge(w_used, U_BO)
            block_squares(lambda i: pair(4 + 2 * i), D, 9, 16)
            hi(u, *range(8, 14))
            transposed(8, lambda n: Q[:, n // 2, (n % 2) * 512:(n % 2) * 512 + 512], 3, range(0, 4), qkt_psum)
            attention("B")
            ht_his(5)
            hi(u, *range(14, 22))

            nc.scalar.activation(wr_hi[:, :], wr[:, :], ACT.Copy).then_inc(wr_hi_ready, 1)
            act.wait_ge(x_new, 6)
            norm_root()
            ht_his(6)
            act.wait_ge(r_shift, 1)
            nc.scalar.activation(rt[:, 3, :], rt[:, 3, :], ACT.Exp).then_inc(r_exp, 1)

            def moe(p):
                steps0 = MOE_STEPS * p
                for b in range(4):
                    act.wait_ge(selt_psum, 4 * p + b + 1)
                    nc.scalar.activation(SELT[:, 2 * b:2 * b + 2, :].rearrange("p e t -> p (e t)"),
                                         PS[:, 3 + b, :], ACT.Copy).then_inc(selt_ready, 1)

                def xt(e, last=None):
                    act.wait_ge(g_psum, e + (N_EXP * p + 1))
                    if not isinstance(e, int):
                        act.wait_ge(w_used, last)
                    nc.scalar.activation(XT_HI.rearrange("p k s -> p (k s)"), pair(5), ACT.Copy
                                         ).then_inc(xt_hi, 1)

                def silu(u, k):
                    act.wait_ge(w_used, u.count(k) + 1)
                    nc.scalar.activation(ESIL, PS[:, 0, :], ACT.Silu).then_inc(e_silu, 1)

                def at(s):
                    act.wait_ge(e_at_psum, s + (steps0 + 1))
                    nc.scalar.activation(AT_HI[:, :], PS[:, 2, :], ACT.Copy).then_inc(e_at_hi, 1)

                def step(u, s):
                    hi(u, *range(0, 7))
                    at(s - 1)
                    hi(u, *range(7, 12))
                    silu(u, 7)

                def y(e, last):
                    act.wait_ge(w_used, last)
                    nc.scalar.activation(Y, pair(3), ACT.Copy).then_inc(ey_ready, 1)

                base = U_MOE + p * MOE_STEPS * E_UNITS
                xt(0)
                hi(Units(base), *range(0 if p else 6, 8))
                base += E_IN
                silu(Units(base), -1)
                with act.Fori(0, N_EXP - 1) as e:
                    with act.Fori(0, E_STEPS - 1) as j:
                        step(Units(base, e * E_STEPS + j, E_UNITS), e * E_STEPS + j + 1)
                    u = Units(base, e * E_STEPS + (E_STEPS - 1), E_UNITS)
                    xt(e + 1, u.count(-E_OUT))
                    step(u, e * E_STEPS + E_STEPS)
                    y(e, u.count(E_UNITS))
                e = N_EXP - 1
                with act.Fori(0, E_STEPS - 1) as j:
                    step(Units(base, e * E_STEPS + j, E_UNITS), j + (e * E_STEPS + 1))
                at(MOE_STEPS - 1)
                hi(Units(base + (MOE_STEPS - 1) * E_UNITS), *range(0, 4))
                y(e, base + (MOE_STEPS - 1) * E_UNITS + E_OUT)

            moe(0)
            with overflow(act):
                moe(1)
                act.nop()

        @block.vector
        def _(dve):
            chain = Chain(dve, dve_chain)
            V_ = nc.vector

            def bc(ap, n):
                return ap.unsqueeze(2).broadcast_to([ap.shape[0], ap.shape[1], n])

            def lo(u, *units):
                for k in units:
                    dve.wait_ge(w_hi, u.count(k) + 1)
                    V_.tensor_tensor(WLO[:, u.split(k), :], WRAW[:, u.raw(k), :],
                                     f32(WHI[:, u.split(k), :]), ALU.subtract).then_inc(w_lo, 1)

            def products(n0, buf, ks):
                for k in ks:
                    dve.wait_ge(ada_landed[k % ADA_SLOTS], ada_rounds(n0, k))
                    if k or not isinstance(n0, int) or n0:
                        dve.wait_ge(ada_used, n0 + k)
                    src, c = ADA[:, k % ADA_SLOTS, :], condT[:, k:k + 1]
                    if k == 0:
                        V_.tensor_scalar(ACC[:, buf, :], src, c, None, ALU.mult).then_inc(ada_used, 1)
                    else:
                        V_.scalar_tensor_tensor(ACC[:, buf, :], src, c, ACC[:, buf, :], ALU.mult, ALU.add
                                                ).then_inc(ada_used, 1)

            def ada_rounds(n0, k):
                return n0 * (16 // ADA_SLOTS) + 16 * (k // ADA_SLOTS + 1)

            roots = [0]

            def await_root():
                roots[0] += 1
                dve.wait_ge(root_ready, roots[0])

            def norm(scale_slot, shift_slot, gains, src_count, fresh=True):
                if fresh:
                    V_.tensor_scalar(nx[:, :, 1:2], nx[:, :, 0:1], 1.0 / D, EPS, ALU.mult, ALU.add
                                     ).then_inc(var_ready, 1)
                    await_root()
                    chain(V_.reciprocal(nx[:, :, 1:2], nx[:, :, 1:2]))
                dve.wait_ge(gain_landed, 16 * gains)
                V_.scalar_tensor_tensor(MOD[:, scale_slot, :], MOD[:, scale_slot, :], 1.0, GB,
                                        ALU.add, ALU.mult).then_inc(gain_used, 1)
                dve.wait_ge(gain_used, gains)
                for i in range(TB):
                    chain(V_.scalar_tensor_tensor(H[:, i, :], X[:, i, :], nx[:, i, 1:2], MOD[:, scale_slot, :],
                                                  ALU.mult, ALU.mult))
                    V_.tensor_tensor(H[:, i, :], H[:, i, :], MOD[:, shift_slot, :], ALU.add
                                     ).then_inc(h_ready, 1)

            def ht_los(use, scale=None):
                for b in range(4):
                    dve.wait_ge(ht_hi, 4 * use + b + 1)
                    dst = HT_LO[:, 2 * b:2 * b + 2, :].rearrange("p k s -> p (k s)")
                    high = f32(HT_HI[:, 2 * b:2 * b + 2, :].rearrange("p k s -> p (k s)"))
                    if scale is None:
                        V_.tensor_tensor(dst, PS[:, b, :], high, ALU.subtract).then_inc(ht_lo, 1)
                    else:
                        V_.scalar_tensor_tensor(dst, PS[:, b, :], scale, high, ALU.mult, ALU.subtract
                                                ).then_inc(ht_lo, 1)

            def head_norm(count, heads, width, src_of, dst_of, done, squares_wide=None):
                for i in range(TB):
                    dve.wait_ge(sq_ready, count + i + 1)
                    chain(V_.tensor_reduce(ss[:, i, 0:heads],
                                           W4[:, 0:heads * width].rearrange("p (h d) -> p h d", h=heads),
                                           axis=AX, op=ALU.add))
                    V_.tensor_scalar(ss[:, i, 0:heads], ss[:, i, 0:heads], 1.0 / width, EPS,
                                     ALU.mult, ALU.add).then_inc(var_ready, 1)
                    await_root()
                    V_.reciprocal(ss[:, i, 0:heads], ss[:, i, 0:heads]).then_inc(sq_read, 1)
                    dve.wait_ge(sq_read, count + i + 1)
                    for dst in dst_of(i):
                        last = V_.tensor_tensor(dst, src_of(i), bc(ss[:, i, 0:heads], width), ALU.mult)
                        last.then_inc(done, 1)

            def attention(a):
                sems = attn[a]

                def biased(n):
                    i, h = n // HEADS, n % HEADS
                    span = (i + 1) * P
                    dve.wait_ge(sems["logits"], n + 1)
                    if n >= 2:
                        dve.wait_ge(sems["pt_psum"], n - 1)
                    b = 2 * (n % 2)
                    V_.tensor_tensor(S[:, n % 2, :, 0:span], PS[:, b:b + 2, 0:span],
                                     BIAS[:, 2 * h:2 * h + 2, 2 * P - span:], ALU.add
                                     ).then_inc(sems["biased"], 1)
                    dve.wait_ge(sems["biased"], n + 1)
                    mx, nm = sm[:, n % 2, 0:2], sm[:, n % 2, 2:4]
                    chain(V_.tensor_reduce(mx, S[:, n % 2, :, 0:span], axis=AX, op=ALU.max))
                    if a == "B":
                        chain(V_.tensor_tensor(mx, mx, sinks[:, 2 * h:2 * h + 2], ALU.max))
                    V_.tensor_scalar(nm, mx, -1.0, None, ALU.mult).then_inc(sems["negmax"], 1)

                def probs(n):
                    span = (n // HEADS + 1) * P
                    dve.wait_ge(sems["expd"], 2 * n + 2)
                    total, r = sm[:, n % 2, 4:6], sm[:, n % 2, 8:10]
                    s0, s1 = S[:, n % 2, 0, 0:span], S[:, n % 2, 1, 0:span]
                    if a == "A":
                        chain(V_.reciprocal(r, total))
                        chain(V_.tensor_tensor(r[:, 1:2], r[:, 1:2], neglam[:, 2:3], ALU.mult))
                        chain(V_.tensor_scalar(s0, s0, r[:, 0:1], None, ALU.mult))
                        V_.scalar_tensor_tensor(s0, s1, r[:, 1:2], s0, ALU.mult, ALU.add
                                                ).then_inc(sems["probs"], 1)
                    else:
                        chain(V_.tensor_tensor(r, total, sm[:, n % 2, 6:8], ALU.add))
                        chain(V_.reciprocal(r, r))
                        V_.tensor_tensor(S[:, n % 2, :, 0:span], S[:, n % 2, :, 0:span], bc(r, span), ALU.mult
                                         ).then_inc(sems["probs"], 1)

                n_all = TB * HEADS
                biased(0)
                for n in range(n_all):
                    if n + 1 < n_all:
                        biased(n + 1)
                    probs(n)

            def residual(banks_of, gate_slot, tmp_of):
                for i in range(TB):
                    chain(V_.tensor_tensor(tmp_of(i), banks_of(i), MOD[:, gate_slot, :], ALU.mult))
                    V_.tensor_tensor(X[:, i, :], X[:, i, :], tmp_of(i), ALU.add).then_inc(x_new, 1)

            def pair(b):
                return PS[:, b:b + 2, :].rearrange("p b n -> p (b n)")

            dve.wait_ge(small_landed, 16 * SMALL)
            lv = lamv.rearrange("p (a b d) -> p a b d", a=2, b=2)
            chain(V_.tensor_tensor(lv[:, :, 0, :], lv[:, :, 0, :], lv[:, :, 1, :], ALU.mult))
            V_.tensor_reduce(neglam[:, 0:2], lv[:, :, 0, :], axis=AX, op=ALU.add).then_inc(sq_read, 1)
            dve.wait_ge(sq_ready, 1)
            chain(V_.tensor_tensor(neglam[:, 2:3], neglam[:, 1:2], neglam[:, 0:1], ALU.subtract))
            chain(V_.tensor_scalar(neglam[:, 2:3], neglam[:, 2:3], -LAM_INIT, None, ALU.add))
            chain(V_.tensor_scalar(gcol[:, 0:1], gcol[:, 0:1], 64 ** -0.5, None, ALU.mult))
            chain(V_.tensor_scalar(gcol[:, 3:4], gcol[:, 3:4], 64 ** -0.5, None, ALU.mult))
            chain(V_.tensor_scalar(gcol[:, 2:3], gcol[:, 2:3], 1.0 - LAM_INIT, None, ALU.mult))

            dve.wait_ge(cond_ready, 1)

            def add_mod0(c):
                dve.wait_ge(mod_sum, 2 * c + 2)
                V_.tensor_tensor(MOD[:, MOD0[c], :], MOD[:, MOD0[c], :], pair(2 * (c % 2)), ALU.add
                                 ).then_inc(mod_ready, 2)

            dve.wait_ge(modb_landed, 16 * 6)
            for c in range(6):
                if c >= 2:
                    dve.wait_ge(mod_sum, 2 * (c - 1))
                products(c * KT, c % 2, range(KT))
                if c >= 1:
                    add_mod0(c - 1)
            add_mod0(5)
            dve.wait_ge(mod_ready, 12)
            dve.wait_ge(x_landed, 16)
            dve.wait_ge(x_squares, 2)
            norm(MOD0[1], MOD0[0], 1, 0)
            ht_los(0)

            u = Units(U_QKV)
            lo(u, *range(0, 14))
            dve.wait_ge(bias_landed, 16)

            def heads_of(ap, h):
                return ap.rearrange("p (h d) -> p h d", h=h)

            head_norm(1, 16, 64, lambda i: heads_of(pair(4 + 2 * i), 16),
                      lambda i: [heads_of(Q[:, i, :], 16)], qk_norm)
            lo(u, *range(14, 20))
            head_norm(3, 16, 64, lambda i: heads_of(pair(2 * i), 16),
                      lambda i: [heads_of(K[:, i, :], 16)], qk_norm)
            lo(u, *range(20, 30))
            dve.wait_ge(bias_masked, 1)
            attention("A")
            dve.wait_ge(attn["A"]["o_ready"], TB * HEADS)
            head_norm(5, 8, P, lambda i: heads_of(Q[:, i, :], 8), lambda i: [heads_of(Q[:, i, :], 8)], h_ready)
            ht_los(1, scale=gcol[:, 2:3])
            lo(u, *range(30, 36))
            dve.wait_ge(w_used, U_FF)
            residual(lambda i: pair(4 + 2 * i), MOD0[2], lambda i: H[:, i, :])
            dve.wait_ge(x_squares, 4)
            norm(MOD0[4], MOD0[3], 2, 1)
            ht_los(2)

            def f_act(n):
                dve.wait_ge(silu_ready, n)
                V_.tensor_tensor(FACT, FSIL, PS[:, 0:2, FC:2 * FC], ALU.mult).then_inc(act_ready, 1)

            def f_at(n):
                dve.wait_ge(at_hi, n)
                V_.tensor_tensor(AT_LO[:, :], PS[:, 2, :], f32(AT_HI[:, :]), ALU.subtract).then_inc(at_ready, 1)

            def add_mod(slot, n):
                half = slot[1]
                dve.wait_ge(mod_sum, n + 1)
                row = MOD[:, bass.ds(slot[0], 1), half * 512:half * 512 + 512].rearrange("p o n -> p (o n)")
                V_.tensor_tensor(row, row, PS[:, 3, :], ALU.add).then_inc(mod_ready, 1)

            f_act(1)
            dve.wait_ge(ht_psum, 12)
            dve.wait_ge(modb_landed, 16 * 14)
            first = U_FF + FF_IN

            def f_pair(it, first, ada):
                u = Units(first, it, RAW_SLOTS) if not isinstance(it, int) else Units(first + it * RAW_SLOTS)
                for b in range(2):
                    for k in range(4):
                        lo(u, 6 * b + k)
                        if ada:
                            products((ada[0] + b) * KT, b, (2 * k, 2 * k + 1))
                    f_at(it * 2 + (b + 1))
                    lo(u, 6 * b + 4, 6 * b + 5)
                    if ada:
                        add_mod((ada[1] + b, 0), (ada[0] + b) * 2)
                    f_act(it * 2 + (b + 2))
                    if ada:
                        add_mod((ada[1] + b, 1), (ada[0] + b) * 2 + 1)

            with dve.Fori(0, 3) as it:
                f_pair(it, first, (it * 2 + 6, it * 2))
            f_pair(3, first, (12, 7))
            f_pair(4, first, None)
            f_at(FF_STEPS)
            u = Units(U_KV - FF_OUT)
            lo(u, *range(0, 6))
            dve.wait_ge(w_used, U_KV)
            residual(lambda i: pair(4 + 2 * i), MOD0[5], lambda i: H[:, i, :])
            dve.wait_ge(x_squares, 6)
            dve.wait_ge(mod_ready, 28)
            norm(MODKV[1], MODKV[0], 3, 2)
            ht_los(3)
            head_norm(7, 4, 64, lambda i: heads_of(PS[:, 4 + i, 0:256], 4),
                      lambda i: [KDUP[:, i, :, c, :] for c in range(2)], kdup_ready)
            dve.wait_ge(ht_psum, 16)
            norm(MOD1[1], MOD1[0], 4, 3, fresh=False)
            ht_los(4)
            u = Units(U_BQ)
            lo(u, *range(0, 8))
            head_norm(9, 16, 64, lambda i: heads_of(pair(4 + 2 * i), 16),
                      lambda i: [heads_of(Q[:, i, :], 16)], qk_norm)
            lo(u, *range(8, 14))
            dve.wait_ge(bias_masked, 4)
            attention("B")
            ht_los(5)
            lo(u, *range(14, 22))
            dve.wait_ge(wr_hi_ready, 1)
            V_.tensor_tensor(wr_lo[:, :], wr[:, :], f32(wr_hi[:, :]), ALU.subtract).then_inc(wr_ready, 1)
            dve.wait_ge(w_used, U_MOE)
            residual(lambda i: pair(4 + 2 * i), MOD1[2], lambda i: H[:, i, :])
            dve.wait_ge(x_squares, 8)
            norm(MOD1[4], MOD1[3], 5, 4)
            ht_los(6)

            def tok_e(n):
                return rt[:, n, :].rearrange("p (i e) -> p i e", i=TB)

            logits, rank, mask, ex, wt, pos = (tok_e(n) for n in range(6))
            small = rt[:, 6, :]
            V_.memset(XACC, 0.0).then_inc(sc_added, 1)
            dve.wait_ge(r_logits, 1)
            chain(V_.tensor_tensor(logits, PS[:, 4, 0:16].rearrange("p (i e) -> p i e", i=TB),
                                   rb[:, :].unsqueeze(1).broadcast_to([P, TB, N_EXP]), ALU.add))
            shape4 = [P, TB, N_EXP, N_EXP]
            above = W4[:, 0:128].rearrange("p (i e f) -> p i e f", i=TB, e=N_EXP)
            equal = W4[:, 128:256].rearrange("p (i e f) -> p i e f", i=TB, e=N_EXP)
            other, own = logits.unsqueeze(2).broadcast_to(shape4), logits.unsqueeze(3).broadcast_to(shape4)
            lower = CST[:, CST_LOWER:].rearrange("p (e f) -> p e f", e=N_EXP).unsqueeze(1).broadcast_to(shape4)
            chain(V_.tensor_tensor(above, other, own, ALU.is_gt))
            chain(V_.tensor_tensor(equal, other, own, ALU.is_equal))
            chain(V_.tensor_tensor(equal, equal, lower, ALU.mult))
            chain(V_.tensor_tensor(above, above, equal, ALU.add))
            chain(V_.tensor_reduce(rank, above, axis=AX, op=ALU.add))
            V_.tensor_scalar(mask, rank, 1.5, None, ALU.is_lt).then_inc(mask_ready, 1)
            chain(V_.tensor_reduce(small[:, 0:2], logits, axis=AX, op=ALU.max))
            V_.tensor_tensor(ex, logits, bc(small[:, 0:2], N_EXP), ALU.subtract).then_inc(r_shift, 1)
            dve.wait_ge(r_exp, 1)
            dve.wait_ge(mask_ready, 1)
            chain(V_.tensor_tensor(ex, ex, mask, ALU.mult))
            chain(V_.tensor_reduce(small[:, 2:4], ex, axis=AX, op=ALU.add))
            chain(V_.reciprocal(small[:, 4:6], small[:, 2:4]))
            chain(V_.tensor_tensor(wt, ex, bc(small[:, 4:6], N_EXP), ALU.mult))
            dve.wait_ge(pos_psum, 1)
            chain(V_.tensor_copy(rt[:, 5, :], PS[:, 5, 0:16]))
            chain(V_.tensor_reduce(small[0:1, 6:7], PS[0:1, 5, 16:24], axis=AX, op=ALU.max))
            V_.tensor_scalar(flag[:, :], small[0:1, 6:7], float(P), None, ALU.is_gt).then_inc(flag_ready, 1)

            def moe(p):
                steps0 = MOE_STEPS * p
                if p:
                    chain(V_.tensor_scalar(rt[:, 5, :], rt[:, 5, :], -float(P), None, ALU.add))
                for e in range(N_EXP):
                    if e >= 4:
                        dve.wait_ge(selt_psum, 4 * p + (e - 4) // 2 + 1)
                    for i in range(TB):
                        at = pos[:, i, e:e + 1]
                        V_.tensor_scalar(SEL[:, e, i, :], iota, at, mask[:, i, e:e + 1], ALU.is_equal, ALU.mult
                                         ).then_inc(sel_ready, 1)
                        V_.tensor_scalar(SELW[:, e % 4, i, :], iota, at, wt[:, i, e:e + 1], ALU.is_equal,
                                         ALU.mult).then_inc(selw_ready, 1)

                def xt(e):
                    dve.wait_ge(xt_hi, e + (N_EXP * p + 1))
                    V_.tensor_tensor(XT_LO.rearrange("p k s -> p (k s)"), pair(5),
                                     f32(XT_HI.rearrange("p k s -> p (k s)")), ALU.subtract).then_inc(xt_ready, 1)

                def act(s):
                    dve.wait_ge(e_silu, s + (steps0 + 1))
                    V_.tensor_tensor(EACT, ESIL, PS[:, 1, :], ALU.mult).then_inc(e_act, 1)

                def at_lo(s):
                    dve.wait_ge(e_at_hi, s + (steps0 + 1))
                    V_.tensor_tensor(AT_LO[:, :], PS[:, 2, :], f32(AT_HI[:, :]), ALU.subtract).then_inc(e_at, 1)

                def step(u, s):
                    lo(u, *range(0, 7))
                    at_lo(s - 1)
                    lo(u, *range(7, 12))
                    act(s)

                def scattered(e):
                    for n in range(4):
                        i, half = n // 2, n % 2
                        dve.wait_ge(sc_psum, e * 4 + (4 * N_EXP * p + n + 1))
                        dve.wait_ge(sc_added, e * 4 + (4 * N_EXP * p + n + 1))
                        row = XACC[:, i, half * 512:half * 512 + 512]
                        V_.tensor_tensor(row, row, PS[:, (7, 3, 4, 7)[n], :], ALU.add).then_inc(sc_added, 1)

                base = U_MOE + p * MOE_STEPS * E_UNITS
                xt(0)
                lo(Units(base), *range(0 if p else 6, 8))
                base += E_IN
                act(0)
                with dve.Fori(0, N_EXP - 1) as e:
                    with dve.Fori(0, E_STEPS - 1) as j:
                        step(Units(base, e * E_STEPS + j, E_UNITS), e * E_STEPS + j + 1)
                    xt(e + 1)
                    step(Units(base, e * E_STEPS + (E_STEPS - 1), E_UNITS), e * E_STEPS + E_STEPS)
                    scattered(e)
                e = N_EXP - 1
                with dve.Fori(0, E_STEPS - 1) as j:
                    step(Units(base, e * E_STEPS + j, E_UNITS), j + (e * E_STEPS + 1))
                at_lo(MOE_STEPS - 1)
                lo(Units(base + (MOE_STEPS - 1) * E_UNITS), *range(0, 4))
                scattered(e)
                dve.wait_ge(sc_added, 4 * N_EXP * (p + 1) + 1)
                if p:
                    dve.wait_ge(out_stored, 32)
                for i in range(TB):
                    chain(V_.tensor_tensor(OUT[:, i, :], XACC[:, i, :], MOD[:, MOD1[5], :], ALU.mult))
                    V_.tensor_tensor(OUT[:, i, :], OUT[:, i, :], X[:, i, :], ALU.add).then_inc(out_ready, 1)

            moe(0)
            with overflow(dve):
                moe(1)
                dve.nop()

        @block.tensor
        def _(pe):
            def mm(out, a, b, start=True, stop=True):
                return nc.tensor.matmul(out, a, b, start=start, stop=stop)

            def split_mm(out, a_hi, a_lo, w_hi_ap, w_lo_ap, start, stop):
                mm(out, a_hi, w_hi_ap, start, False)
                mm(out, a_hi, w_lo_ap, False, False)
                return mm(out, a_lo, w_hi_ap, False, stop)

            def split_ready(u, k):
                pe.wait_ge(w_lo, u.count(k) + 1)

            def project(u, k0, bank):
                for k in range(KT):
                    split_ready(u, k0 + k)
                    s = u.split(k0 + k)
                    for i in range(TB):
                        rows = slice(i * P, i * P + P)
                        for half in range(2):
                            cols = slice(half * 512, half * 512 + 512)
                            last = split_mm(PS[:, bank + 2 * i + half, :], HT_HI[:, k, rows], HT_LO[:, k, rows],
                                            WHI[:, s, cols], WLO[:, s, cols], k == 0, k == KT - 1)
                    last.then_inc(w_used, 1)

            def ht_transposes(src):
                for b in range(4):
                    for k in (2 * b, 2 * b + 1):
                        for i in range(TB):
                            at = (k % 2) * 256 + i * P
                            last = nc.tensor.transpose(PS[:, b, at:at + P], src[:, i, k * P:(k + 1) * P], ident)
                    last.then_inc(ht_psum, 1)

            def block_transposes(src, first_bank, total):
                for n in range(4):
                    i, hb = n // 2, n % 2
                    for h in range(4):
                        c = hb * 512 + h * P
                        last = nc.tensor.transpose(PS[:, first_bank + n, h * P:(h + 1) * P],
                                                   src[:, i, c:c + P], ident)
                    last.then_inc(total, 1)

            def attention(a):
                sems = attn[a]

                def logits(n):
                    i, h = n // HEADS, n % HEADS
                    if n >= 2:
                        pe.wait_ge(sems["biased"], n - 1)
                    for m in range(2):
                        rows = slice(m * 64, m * 64 + 64)
                        if a == "A":
                            keys = K[rows, 0:i + 1, h * P:(h + 1) * P]
                        else:
                            keys = KBT[rows, h // 2, 0:(i + 1) * P]
                        last = mm(PS[:, 2 * (n % 2) + m, 0:(i + 1) * P], Q[rows, i, h * P:(h + 1) * P], keys)
                    last.then_inc(sems["logits"], 1)

                def transposes(n):
                    i = n // HEADS
                    pe.wait_ge(sems["probs"], n + 1)
                    if n >= 2:
                        pe.wait_ge(sems["pt_ready"], n - 1)
                    for m in range(1 if a == "A" else 2):
                        for kt in range(i + 1):
                            at = m * 256 + kt * P
                            last = nc.tensor.transpose(PS[:, 4 + n % 2, at:at + P],
                                                       S[:, n % 2, m, kt * P:(kt + 1) * P], ident)
                    last.then_inc(sems["pt_psum"], 1)

                def products(n):
                    i, h = n // HEADS, n % HEADS
                    pe.wait_ge(sems["pt_ready"], n + 1)
                    if n >= 2:
                        pe.wait_ge(sems["o_ready"], n - 1)
                    bank = 6 + n % 2
                    if a == "A":
                        for kt in range(i + 1):
                            last = mm(PS[:, bank, 0:P], PT[:, n % 2, 0, kt * P:(kt + 1) * P],
                                      V[:, kt, h * P:(h + 1) * P], kt == 0, kt == i)
                    else:
                        j = h // 2
                        for m in range(2):
                            for kt in range(i + 1):
                                last = mm(PS[:, bank, m * 64:(m + 1) * 64], PT[:, n % 2, m, kt * P:(kt + 1) * P],
                                          KV[:, kt, 256 + j * 64:256 + (j + 1) * 64], kt == 0, kt == i)
                    last.then_inc(sems["pv"], 1)

                n_all = TB * HEADS
                logits(0)
                logits(1)
                for n in range(n_all):
                    transposes(n)
                    if n + 2 < n_all:
                        logits(n + 2)
                    products(n)

            pe.wait_ge(small_landed, 16 * SMALL)
            for h in range(NBIAS):
                if h >= 4:
                    pe.wait_ge(toep_sbuf, h - 3)
                mm(PS[:, 4 + h % 4, 0:SPAN], relb[:, h:h + 1].broadcast_to([32, P]), onehot).then_inc(toep_mm, 1)
            pe.wait_ge(cst_landed, 16)

            for c in range(6):
                pe.wait_ge(ada_used, KT * (c + 1))
                if c >= 2:
                    pe.wait_ge(mod_ready, 2 * (c - 1))
                for half in range(2):
                    mm(PS[:, 2 * (c % 2) + half, :], ones, ACC[:, c % 2, half * 512:half * 512 + 512]
                       ).then_inc(mod_sum, 1)

            u = Units(U_QKV)
            pe.wait_ge(mod_ready, 12)
            pe.wait_ge(h_ready, 2)
            ht_transposes(H)
            pe.wait_ge(ht_lo, 4)
            pe.wait_ge(toep_sbuf, NBIAS)
            project(u, 0, 4)
            project(u, KT, 0)
            pe.wait_ge(qk_norm, 2)
            project(u, 2 * KT, 4)
            pe.wait_ge(qk_norm, 4)
            block_transposes(Q, 0, qkt_psum)
            pe.wait_ge(v_copied, 2)
            block_transposes(K, 4, qkt_psum)
            pe.wait_ge(qkt_ready, 8)
            attention("A")
            pe.wait_ge(h_ready, 4)
            ht_transposes(Q)
            pe.wait_ge(ht_lo, 8)
            project(Units(U_WO), 0, 4)
            pe.wait_ge(h_ready, 6)
            ht_transposes(H)
            pe.wait_ge(ht_lo, 12)

            def f_in(u, k0, ks, first, last):
                for k in ks:
                    split_ready(u, k0 + k)
                    s = u.split(k0 + k)
                    for kt in range(2):
                        cols, kk = slice(kt * 512, kt * 512 + 512), 2 * k + kt
                        for i in range(TB):
                            rows = slice(i * P, i * P + P)
                            x = split_mm(PS[:, i, :], HT_HI[:, kk, rows], HT_LO[:, kk, rows], WHI[:, s, cols],
                                         WLO[:, s, cols], kk == 0, kk == KT - 1)
                    x.then_inc(w_used, 1)

            def f_transposes(n):
                pe.wait_ge(act_ready, n)
                for c in range(2):
                    for i in range(TB):
                        last = nc.tensor.transpose(PS[:, 2, c * 256 + i * P:c * 256 + i * P + P],
                                                   FACT[:, i, c * P:(c + 1) * P], ident)
                last.then_inc(at_psum, 1)

            def f_out(u, k0, c, start, stop):
                split_ready(u, k0)
                s = u.split(k0)
                for i in range(TB):
                    rows = slice(c * 256 + i * P, c * 256 + i * P + P)
                    for half in range(2):
                        cols = slice(half * 512, half * 512 + 512)
                        last = split_mm(PS[:, 4 + 2 * i + half, :], AT_HI[:, rows], AT_LO[:, rows],
                                        WHI[:, s, cols], WLO[:, s, cols], start, stop)
                last.then_inc(w_used, 1)
                return last

            def mod_half(chunk, buf, half):
                if half == 0:
                    pe.wait_ge(ada_used, (chunk + 1) * KT)
                pe.wait_ge(mod_ready, chunk * 2 + half)
                mm(PS[:, 3, :], ones, ACC[:, buf, half * 512:half * 512 + 512]).then_inc(mod_sum, 1)

            u = Units(U_FF)
            f_in(u, 0, range(4), True, False)
            first = U_FF + FF_IN

            def f_pair(it, ada, clears):
                u = Units(first, it, RAW_SLOTS) if not isinstance(it, int) else Units(first + it * RAW_SLOTS)
                for b in range(2):
                    pe.wait_ge(act_ready, it * 2 + (b + 1))
                    f_in(u, 6 * b, (0, 1), True, False)
                    f_transposes(it * 2 + (b + 1))
                    f_in(u, 6 * b, (2, 3), True, False)
                    if ada is not None:
                        mod_half(ada + b, b, 0)
                    pe.wait_ge(at_ready, it * 2 + (b + 1))
                    f_out(u, 6 * b + 4, 0, clears and b == 0, False)
                    if ada is not None:
                        mod_half(ada + b, b, 1)
                    f_out(u, 6 * b + 5, 1, False, False)

            f_pair(0, 6, True)
            with pe.Fori(1, 3) as it:
                f_pair(it, it * 2 + 6, False)
            f_pair(3, 12, False)
            f_pair(4, None, False)
            u = Units(U_KV - FF_OUT)
            f_transposes(FF_STEPS)
            pe.wait_ge(at_ready, FF_STEPS)
            f_out(u, 0, 0, False, False)
            f_out(u, 1, 1, False, True)

            pe.wait_ge(h_ready, 8)
            ht_transposes(H)
            pe.wait_ge(ht_lo, 16)
            u = Units(U_KV)
            for k in range(KT // 2):
                split_ready(u, k)
                s = u.split(k)
                for kt in range(2):
                    cols, kk = slice(kt * 512, kt * 512 + 512), 2 * k + kt
                    for i in range(TB):
                        rows = slice(i * P, i * P + P)
                        last = split_mm(PS[:, 4 + i, :], HT_HI[:, kk, rows], HT_LO[:, kk, rows], WHI[:, s, cols],
                                        WLO[:, s, cols], kk == 0, kk == KT - 1)
                last.then_inc(w_used, 1)
            pe.wait_ge(h_ready, 10)
            ht_transposes(H)
            pe.wait_ge(ht_lo, 20)
            pe.wait_ge(kdup_ready, 4)
            project(Units(U_BQ), 0, 4)
            for b in range(2):
                for j in (2 * b, 2 * b + 1):
                    for i in range(TB):
                        at = (j % 2) * 256 + i * P
                        last = nc.tensor.transpose(PS[:, b, at:at + P],
                                                   KDUP[:, i, j, :, :].rearrange("p c d -> p (c d)"), ident)
                last.then_inc(kbt_psum, 1)
            pe.wait_ge(qk_norm, 6)
            pe.wait_ge(kbt_ready, 2)
            block_transposes(Q, 0, qkt_psum)
            pe.wait_ge(qkt_ready, 12)
            attention("B")
            pe.wait_ge(attn["B"]["o_ready"], TB * HEADS)
            ht_transposes(Q)
            pe.wait_ge(ht_lo, 24)
            project(Units(U_BO), 0, 4)
            pe.wait_ge(h_ready, 12)
            ht_transposes(H)
            pe.wait_ge(ht_lo, 28)

            pe.wait_ge(wr_ready, 1)
            for i in range(TB):
                rows = slice(i * P, i * P + P)
                for k in range(KT):
                    e = slice(k * N_EXP, (k + 1) * N_EXP)
                    last = split_mm(PS[:, 4, i * N_EXP:(i + 1) * N_EXP], HT_HI[:, k, rows], HT_LO[:, k, rows],
                                    wr_hi[:, e], wr_lo[:, e], k == 0, k == KT - 1)
            last.then_inc(r_logits, 1)
            pe.wait_ge(mask_ready, 1)
            m0, m1 = rt[:, 2, 0:N_EXP], rt[:, 2, N_EXP:2 * N_EXP]
            mm(PS[:, 5, 0:8], tri, m0)
            mm(PS[:, 5, 8:16], ones, m0, True, False)
            mm(PS[:, 5, 8:16], tri, m1, False, True)
            mm(PS[:, 5, 16:24], ones, m0, True, False)
            mm(PS[:, 5, 16:24], ones, m1, False, True).then_inc(pos_psum, 1)

            def moe(p):
                steps0 = MOE_STEPS * p
                pe.wait_ge(flag_ready, 1)
                if p:
                    pe.wait_ge(sc_added, 4 * N_EXP + 1)
                for e in range(N_EXP):
                    pe.wait_ge(selw_ready, 2 * N_EXP * p + TB * (e + 1))
                    for i in range(TB):
                        at = (e % 2) * 256 + i * P
                        last = nc.tensor.transpose(PS[:, 3 + e // 2, at:at + P], SELW[:, e % 4, i, :], ident)
                    if e % 2:
                        last.then_inc(selt_psum, 1)
                pe.wait_ge(sel_ready, 2 * N_EXP * (p + 1))
                pe.wait_ge(selt_ready, 4 * (p + 1))

                def gather(e):
                    for k in range(KT):
                        out = PS[:, 5 + k // 4, (k % 4) * P:(k % 4) * P + P]
                        for i in range(TB):
                            sel = SEL[:, e, i, :] if isinstance(e, int) else SEL[
                                :, bass.ds(e, 1), i, :].rearrange("p o s -> p (o s)")
                            last = mm(out, H[:, i, k * P:(k + 1) * P], sel, i == 0, i == 1)
                    last.then_inc(g_psum, 1)

                def e_in(u, ks):
                    for k in ks:
                        split_ready(u, k)
                        s = u.split(k)
                        start, stop = k == 0, k == KT - 1
                        gate, up = slice(0, 512), slice(512, 1024)
                        xh, xl = XT_HI[:, k, :], XT_LO[:, k, :]
                        mm(PS[:, 0, :], xh, WHI[:, s, gate], start, False)
                        mm(PS[:, 0, :], xh, WLO[:, s, gate], False, False)
                        mm(PS[:, 1, :], xh, WHI[:, s, up], start, False)
                        mm(PS[:, 1, :], xh, WLO[:, s, up], False, False)
                        mm(PS[:, 0, :], xl, WHI[:, s, gate], False, stop)
                        last = mm(PS[:, 1, :], xl, WHI[:, s, up], False, stop)
                        last.then_inc(w_used, 1)

                def e_transposes(s):
                    pe.wait_ge(e_act, s + (steps0 + 1))
                    for c in range(4):
                        last = nc.tensor.transpose(PS[:, 2, c * P:(c + 1) * P], EACT[:, c * P:(c + 1) * P], ident)
                    last.then_inc(e_at_psum, 1)

                def e_out(u, k0, s, start, stop):
                    pe.wait_ge(e_at, s + (steps0 + 1))
                    for c in range(4):
                        split_ready(u, k0 + c)
                        slot, rows = u.split(k0 + c), slice(c * P, (c + 1) * P)
                        for half in range(2):
                            cols = slice(half * 512, half * 512 + 512)
                            last = split_mm(PS[:, 3 + half, :], AT_HI[:, rows], AT_LO[:, rows],
                                            WHI[:, slot, cols], WLO[:, slot, cols],
                                            start and c == 0, stop and c == 3)
                        last.then_inc(w_used, 1)

                def step(u, s, start, stop):
                    pe.wait_ge(e_act, s + steps0)
                    e_in(u, range(0, 4))
                    e_transposes(s - 1)
                    e_in(u, range(4, 8))
                    e_out(u, 8, s - 1, start, stop)

                def scatter(e):
                    pe.wait_ge(ey_ready, e + (N_EXP * p + 1))
                    pe.wait_ge(selt_cur, e + (N_EXP * p + 1))
                    for n in range(4):
                        i, half = n // 2, n % 2
                        if n == 3:
                            pe.wait_ge(sc_added, e * 4 + (4 * N_EXP * p + 2))
                        mm(PS[:, (7, 3, 4, 7)[n], :], SELT_CUR[:, i * P:(i + 1) * P],
                           Y[:, half * 512:half * 512 + 512]).then_inc(sc_psum, 1)

                base = U_MOE + p * MOE_STEPS * E_UNITS
                gather(0)
                pe.wait_ge(xt_ready, N_EXP * p + 1)
                e_in(Units(base), range(0, 8))
                base += E_IN

                def expert(e):
                    if not (isinstance(e, int) and e == N_EXP - 1):
                        gather(e + 1)
                    turn = e * E_STEPS
                    u = Units(base, turn, E_UNITS) if not isinstance(e, int) else Units(base + turn * E_UNITS)
                    pe.wait_ge(sc_added, e * 4 + (4 * N_EXP * p + 1))
                    step(u, turn + 1, True, False)
                    with pe.Fori(1, E_STEPS - 1) as j:
                        step(Units(base, turn + j, E_UNITS), j + (turn + 1), False, False)

                with pe.Fori(0, N_EXP - 1) as e:
                    expert(e)
                    pe.wait_ge(xt_ready, e + (N_EXP * p + 2))
                    u = Units(base, e * E_STEPS + (E_STEPS - 1), E_UNITS)
                    step(u, e * E_STEPS + E_STEPS, False, True)
                    scatter(e)
                e = N_EXP - 1
                expert(e)
                u = Units(base + (MOE_STEPS - 1) * E_UNITS)
                e_transposes(MOE_STEPS - 1)
                e_out(u, 0, MOE_STEPS - 1, False, True)
                scatter(e)

            moe(0)
            with overflow(pe):
                moe(1)
                pe.nop()


_INS = ["x", "c", "ada_w", "ada_b", "norm_attn", "norm_ffn", "rel_bias", "a_w_qkv", "a_q_norm", "a_k_norm",
        "a_lambda", "a_subln", "a_w_o", "kv_ada_w", "kv_ada_b", "kv_norm", "kv_w", "kv_k_norm", "b_w_q",
        "b_q_norm", "b_sinks", "b_w_o", "ffn_w_in", "ffn_w_out", "moe_router_w", "moe_router_b", "moe_w_in",
        "moe_w_out"]


def t5_bucket(rel):
    nb = 16
    ret = (rel > 0).astype(np.int32) * nb
    n = np.abs(rel)
    exact = nb // 2
    large = exact + (np.log(np.maximum(n, 1) / exact) / np.log(128 / exact) * (nb - exact)).astype(np.int32)
    return ret + np.where(n < exact, n, np.minimum(large, nb - 1))


def constants():
    cst = np.zeros((P, CST_COLS), np.float32)
    r = np.arange(P)
    cst[:, CST_IDENT:CST_IDENT + P] = r[:, None] == r[None, :]
    cst[:, CST_TRI:CST_TRI + P] = r[:, None] < r[None, :]
    cst[:, CST_IOTA:CST_IOTA + P] = r[None, :]
    cst[:, CST_ONES:CST_ONES + P] = 1.0
    e = np.arange(N_EXP)
    cst[:, CST_LOWER:] = (e[None, :] < e[:, None]).astype(np.float32).reshape(1, -1)
    onehot = np.zeros((32, SPAN), np.float32)
    i = np.arange(SPAN)
    onehot[t5_bucket(i - 255), i] = 1.0
    return cst, onehot


def kernel(**inputs):
    import concourse.bacc as _bacc
    from concourse.bass_utils import run_bass_kernel_spmd as _run

    nc = _bacc.Bacc("TRN2", target_bir_lowering=False, num_devices=1)
    arrays, t = {}, {}
    data = {n: inputs[n] for n in _INS}
    data["cst"], data["onehot"] = constants()
    for name, value in data.items():
        a = np.ascontiguousarray(value)
        arrays[f"in_{name}"] = a
        t[name] = nc.dram_tensor(f"in_{name}", a.shape, mybir.dt.from_np(a.dtype), kind="ExternalInput").ap()
    t["out"] = nc.dram_tensor("out_x", inputs["x"].shape, F32, kind="ExternalOutput").ap()
    trunk(nc, t)
    r = _run(nc, [arrays], core_ids=[0])
    return r.results[0]["out_x"]
```

```python
import math
from contextlib import ExitStack

import concourse.bass as bass
import numpy as np
from concourse import mybir

ALU = mybir.AluOpType
ACT = mybir.ActivationFunctionType
AX = mybir.AxisListType.X
F32 = mybir.dt.float32
F32R = mybir.dt.float32r
I32 = mybir.dt.int32

P = 128
D = 1024
KT = D // P
TB = 2
UNIT = 1024
RAW_SLOTS = 12
SPLIT_SLOTS = 6
ADA_SLOTS = 4
HEADS = 8
NBIAS = 16
D_FF = 2816
FC = 256
FF_STEPS = D_FF // FC
N_EXP = 8
D_EXP = 3584
EC = 512
E_STEPS = D_EXP // EC
EPS = 1e-6
NEG = -1e30
LAM_INIT = 0.8 - 0.6 * math.exp(-0.3 * 0)
SPAN = 3 * P

S_BUFS = 4

TOEP_SLOTS = 2 * (TB * D // SPAN)

U_QKV = 0
U_WO = U_QKV + 3 * KT
U_FF = U_WO + KT
FF_IN = KT // 2
FF_OUT = FC // P
U_KV = U_FF + FF_STEPS * (FF_IN + FF_OUT)
U_BQ = U_KV + KT // 2
U_BO = U_BQ + KT
U_MOE = U_BO + KT
E_IN = KT
E_OUT = EC // P
E_UNITS = E_IN + E_OUT
MOE_STEPS = N_EXP * E_STEPS
U_END = U_MOE + MOE_STEPS * E_UNITS

MOD0 = (0, 1, 2, 3, 4, 6)
MOD1 = (0, 1, 2, 3, 4, 5)
MODKV = (7, 8)
ADA_EARLY = 5
ADA_LATE = 6 + 2
ADA_CHUNKS = 6 + ADA_LATE
S_SPARE = {"A": 5, "B": 0}

CST_IDENT, CST_TRI, CST_IOTA, CST_ONES, CST_LOWER = 0, 128, 256, 384, 512
CST_COLS = 512 + N_EXP * N_EXP


class Units:

    def __init__(self, first, turn=0, per_turn=0):
        assert per_turn % RAW_SLOTS == 0
        self.first, self.turn, self.per = first, turn, per_turn

    def raw(self, k):
        return (self.first + k) % RAW_SLOTS

    def split(self, k):
        return (self.first + k) % SPLIT_SLOTS

    def count(self, k):
        return self.turn * self.per + (self.first + k) if self.per else self.first + k

    def landed(self, k):
        n = 16 * ((self.first + k) // RAW_SLOTS + 1)
        return self.turn * (16 * self.per // RAW_SLOTS) + n if self.per else n


class Chain:

    def __init__(self, engine, sem):
        self.engine, self.sem, self.n, self.base = engine, sem, 0, None

    def __call__(self, instruction):
        instruction.then_inc(self.sem, 1)
        self.n += 1
        self.engine.wait_ge(self.sem, self.n if self.base is None else self.base + self.n)


def chunk_dynamic(turn):
    return not isinstance(turn, int)


def trunk(nc, t):
    ctx = ExitStack()
    with ctx:
        def sb(name, shape, dtype=F32):
            return ctx.enter_context(nc.sbuf_tensor(name, shape, dtype))

        def sem(name):
            return ctx.enter_context(nc.semaphore(name))

        WRAW = sb("WRAW", [P, RAW_SLOTS, UNIT])
        WHI = sb("WHI", [P, SPLIT_SLOTS, UNIT], F32R)
        WLO = sb("WLO", [P, SPLIT_SLOTS, UNIT], F32R)
        MOD = sb("MOD", [P, 9, D])
        SHR = sb("SHR", [P, 4 * D])
        X = sb("X", [P, TB, D])
        H = sb("H", [P, TB, D])
        HT_HI = sb("HT_HI", [P, KT, TB * P], F32R)
        HT_LO = sb("HT_LO", [P, KT, TB * P], F32R)
        Q = sb("Q", [P, TB, D])
        AT_HI = sb("AT_HI", [P, 512], F32R)
        AT_LO = sb("AT_LO", [P, 512], F32R)
        W4 = sb("W4", [P, D])
        S = sb("S", [P, 2, 2, 256])
        CST = sb("CST", [P, CST_COLS])
        condT = sb("condT", [P, KT])
        gcol = sb("gcol", [P, 8])
        lamv = W4[:, 0:256]
        relb = sb("relb", [32, NBIAS])
        sinks = sb("sinks", [P, NBIAS])
        wr = sb("wr", [P, KT * N_EXP])
        wr_hi = sb("wr_hi", [P, KT * N_EXP], F32R)
        wr_lo = sb("wr_lo", [P, KT * N_EXP], F32R)
        rb = sb("rb", [P, N_EXP])
        ss = sb("ss", [P, TB, 16])
        nx = sb("nx", [P, TB, 2])
        sm = sb("sm", [P, S_BUFS, 16])
        neglam = sb("neglam", [P, 4])
        rt = sb("rt", [P, 8, TB * N_EXP])
        flag = sb("flag", [1, 1], I32)
        PS = ctx.enter_context(nc.psum_tensor("PS", [P, 8, 512], F32))
        TOEP = nc.dram_tensor("toep_rows", (NBIAS, P, SPAN), F32)

        ident = CST[:, CST_IDENT:CST_IDENT + P]
        tri = CST[:, CST_TRI:CST_TRI + P]
        iota = CST[:, CST_IOTA:CST_IOTA + P]
        ones = CST[:, CST_ONES:CST_ONES + P]
        ADA = SHR[:, :].rearrange("p (s n) -> p s n", s=ADA_SLOTS)
        BIAS = SHR[:, :].rearrange("p (h k) -> p h k", h=NBIAS)
        GB = S[:, :, :, :].rearrange("p a b k -> p (a b k)")
        K = MOD[:, 7:9, :]
        V = H
        onehot = W4[0:32, 512:512 + SPAN]
        PT = W4[:, :].rearrange("p (n m k) -> p n m k", n=2, m=2)

        def s_buf(a, n):
            if n % S_BUFS < 2:
                return S[:, n % S_BUFS, :, :]
            return MOD[:, S_SPARE[a], :].rearrange("p (n m k) -> p n m k", n=2, m=2)[:, n % 2, :, :]

        def toep_rows(h):
            j = h % TOEP_SLOTS
            place = (Q if j < TOEP_SLOTS // 2 else K)[:, :, :].rearrange("p i n -> p (i n)")
            j %= TOEP_SLOTS // 2
            return place[:, j * SPAN:(j + 1) * SPAN]

        FSIL = Q[:, 0, 0:512].rearrange("p (i f) -> p i f", i=TB)
        FACT = Q[:, 0, 512:1024].rearrange("p (i f) -> p i f", i=TB)
        KBT = MOD[:, 7, :].rearrange("p (j k) -> p j k", j=4)
        KV = MOD[:, 8, :].rearrange("p (i n) -> p i n", i=TB)
        KDUP = MOD[:, 6, :].rearrange("p (i j c d) -> p i j c d", i=TB, j=4, c=2)
        SEL = SHR[:, 0:2048].rearrange("p (e i s) -> p e i s", e=N_EXP, i=TB)
        by_expert = W4[0:N_EXP, 512:512 + TB * P]
        XACC = MOD[:, 0:2, :]
        Y = MOD[:, 2, :]
        EACT = MOD[:, 3, 0:512]
        ESIL = MOD[:, 4, 0:512]
        SELT_CUR = MOD[:, 6, 0:256]
        OUT = MOD[:, 7:9, :]
        SELW = OUT.rearrange("p a (e i s) -> p (a e) i s", i=TB, s=P)
        SELW_CUR = MOD[:, 6, 256:512]
        XT_HI = HT_HI[:, 0:4, :].rearrange("p a (b s) -> p (a b) s", b=2)
        XT_LO = HT_LO[:, 0:4, :].rearrange("p a (b s) -> p (a b) s", b=2)

        def f32(ap):
            return ap.bitcast(F32)

        w_landed = [sem(f"w_landed{r}") for r in range(RAW_SLOTS)]
        w_landed_b = [sem(f"w_landed_b{r}") for r in range(RAW_SLOTS)]
        w_hi = sem("w_hi")
        w_lo = sem("w_lo")
        w_used = sem("w_used")
        ada_landed = [sem(f"ada_landed{r}") for r in range(ADA_SLOTS)]
        ada_used = sem("ada_used")
        mod_sum = sem("mod_sum")
        mod_ready = sem("mod_ready")
        x_landed = sem("x_landed")
        c_landed = sem("c_landed")
        cst_landed = sem("cst_landed")
        small_landed = sem("small_landed")
        mod_clear = sem("mod_clear")
        mod_cleared = sem("mod_cleared")
        modb_first = sem("modb_first")
        modb_landed = sem("modb_landed")
        gain_first = sem("gain_first")
        gain_landed = sem("gain_landed")
        toep_in = sem("toep_in")
        toep_mm = sem("toep_mm")
        toep_sbuf = sem("toep_sbuf")
        toep_dram = [sem(f"toep_dram{j}") for j in range(TOEP_SLOTS)]
        bias_landed = sem("bias_landed")
        cond_ready = sem("cond_ready")
        gain_used = sem("gain_used")
        sq_ready = sem("sq_ready")
        var_ready = sem("var_ready")
        root_ready = sem("root_ready")
        sq_read = sem("sq_read")
        h_ready = sem("h_ready")
        ht_psum = sem("ht_psum")
        ht_hi = sem("ht_hi")
        ht_lo = sem("ht_lo")
        qk_norm = sem("qk_norm")
        v_copied = sem("v_copied")
        qkt_psum = sem("qkt_psum")
        qkt_ready = sem("qkt_ready")
        bias_masked = sem("bias_masked")
        attn = {}
        for a in "AB":
            attn[a] = {n: sem(f"{n}_{a}") for n in (
                "logits", "biased", "negmax", "expd", "probs", "pt_psum", "pt_ready", "pv", "o_ready")}
        x_new = sem("x_new")
        silu_ready = sem("silu_ready")
        act_ready = sem("act_ready")
        at_psum = sem("at_psum")
        at_hi = sem("at_hi")
        at_ready = sem("at_ready")
        kv_ready = sem("kv_ready")
        kdup_ready = sem("kdup_ready")
        kbt_psum = sem("kbt_psum")
        kbt_ready = sem("kbt_ready")
        wr_hi_ready = sem("wr_hi_ready")
        wr_ready = sem("wr_ready")
        r_by_expert = sem("r_by_expert")
        r_sbuf = sem("r_sbuf")
        r_logits = sem("r_logits")
        r_shift = sem("r_shift")
        r_exp = sem("r_exp")
        mask_ready = sem("mask_ready")
        pos_psum = sem("pos_psum")
        flag_ready = sem("flag_ready")
        selw_ready = sem("selw_ready")
        selw_cur = sem("selw_cur")
        selt_psum = sem("selt_psum")
        sel_ready = sem("sel_ready")
        g_psum = sem("g_psum")
        xt_hi = sem("xt_hi")
        xt_ready = sem("xt_ready")
        e_silu, e_act = sem("e_silu"), sem("e_act")
        e_at_psum, e_at_hi, e_at = sem("e_at_psum"), sem("e_at_hi"), sem("e_at")
        ey_ready = sem("ey_ready")
        selt_cur = sem("selt_cur")
        sc_psum = sem("sc_psum")
        sc_added = sem("sc_added")
        out_ready, out_stored = sem("out_ready"), sem("out_stored")
        dve_chain = sem("dve_chain")
        x_squares = sem("x_squares")

        x_v = t["x"].rearrange("b (i p) d -> p (b i) d", p=P)
        out_v = t["out"].rearrange("b (i p) d -> p (b i) d", p=P)
        ffin_v = t["ffn_w_in"].rearrange("l (u k p) (c f) -> (l u) p k c f", k=2, p=P, c=2)
        ein_v = t["moe_w_in"].rearrange("l e (k p) (c j f) -> (l e) j k p c f", p=P, c=2, j=E_STEPS)
        eout_v = t["moe_w_out"].rearrange("l e (s p) d -> (l e s) p d", p=P)
        kvw_v = t["kv_w"].rearrange("(u k p) n -> u p k n", k=2, p=P)
        SMALL = 13

        def overflow(engine):
            engine.wait_ge(flag_ready, 1)
            over = engine.value_load(flag[0:1, 0:1], min_val=0, max_val=1)
            return engine.If(over > 0)

        block = ctx.enter_context(nc.Block())

        @block.sync
        def _(sp):
            with nc.allow_non_contiguous_dma(reason="short rows of c"):
                sp.dma_start(condT[:, :], t["c"].rearrange("b (p k) -> p (b k)", p=P)).then_inc(c_landed, 16)
            sp.wait_ge(mod_clear, 1)
            sp.dma_start(MOD[0:1, 0:2, :], t["ada_b"][0:1, 0:2 * D].rearrange("o (c n) -> o c n", c=2)
                         ).then_inc(modb_first, 16)
            sp.dma_start(X[:, :, :], x_v).then_inc(x_landed, 16)
            sp.dma_start(CST[:, :], t["cst"]).then_inc(cst_landed, 16)
            sp.wait_ge(ada_used, 2 * KT - 1)

            def load(u, k, src, first_round=False, dst_shape=None):
                if not first_round:
                    sp.wait_ge(w_lo, u.count(k - RAW_SLOTS) + 1)
                dst = WRAW[:, u.raw(k), :]
                if dst_shape is not None:
                    dst = dst.rearrange(*dst_shape[0], **dst_shape[1])
                sp.dma_start(dst, src).then_inc(w_landed[u.raw(k)], 16)

            u = Units(U_QKV)
            for g in range(3):
                for k in range(KT):
                    n = g * KT + k
                    load(u, n, t["a_w_qkv"][0, k * P:(k + 1) * P, g * D:(g + 1) * D], n < RAW_SLOTS)
            u = Units(U_WO)
            for k in range(KT):
                load(u, k, t["a_w_o"][0, k * P:(k + 1) * P, :])

            def ff_load_in(u, k0, s):
                for k in range(FF_IN):
                    sp.wait_ge(w_lo, u.count(k0 + k - RAW_SLOTS) + 1)
                    r = u.raw(k0 + k)
                    for kt, landed in enumerate((w_landed[r], w_landed_b[r])):
                        sp.dma_start(WRAW[:, r, kt * 512:kt * 512 + 512].rearrange("p (c f) -> p c f", c=2),
                                     ffin_v[k][:, kt, :, bass.ds(s * FC, FC)]).then_inc(landed, 16)

            def ff_load_out(u, k0, s):
                for k in range(FF_OUT):
                    load(u, k0 + k, t["ffn_w_out"][0, bass.ds(s * FC + k * P, P), :])

            ff_load_in(Units(U_FF), 0, 0)
            first = U_FF + FF_IN
            with sp.Fori(0, (FF_STEPS - 1) // 2) as it:
                u = Units(first, it, RAW_SLOTS)
                for b in range(2):
                    ff_load_in(u, 6 * b, it * 2 + (b + 1))
                    ff_load_out(u, 6 * b + FF_IN, it * 2 + b)
            ff_load_out(Units(U_KV - FF_OUT), 0, FF_STEPS - 1)

            u = Units(U_KV)
            for k in range(KT // 2):
                load(u, k, kvw_v[k], dst_shape=(("p (k n) -> p k n",), dict(k=2)))
            for base, w in ((U_BQ, t["b_w_q"]), (U_BO, t["b_w_o"])):
                u = Units(base)
                for k in range(KT):
                    load(u, k, w[0, k * P:(k + 1) * P, :])

            def e_load_in(u, k0, e, j):
                for k in range(E_IN):
                    load(u, k0 + k, ein_v[e][j][k],
                         dst_shape=(("p (c f) -> p c f",), dict(c=2)))

            def e_load_out(u, k0, s):
                for k in range(E_OUT):
                    load(u, k0 + k, eout_v[s * E_OUT + k])

            def moe_loads(p):
                base = U_MOE + p * MOE_STEPS * E_UNITS
                e_load_in(Units(base), 0, 0, 0)
                base += E_IN
                with sp.Fori(0, N_EXP - 1) as e:
                    with sp.Fori(0, E_STEPS - 1) as j:
                        u = Units(base, e * E_STEPS + j, E_UNITS)
                        e_load_in(u, 0, e, j + 1)
                        e_load_out(u, E_IN, e * E_STEPS + j)
                    u = Units(base, e * E_STEPS + (E_STEPS - 1), E_UNITS)
                    e_load_in(u, 0, e + 1, 0)
                    e_load_out(u, E_IN, e * E_STEPS + (E_STEPS - 1))
                e = N_EXP - 1
                with sp.Fori(0, E_STEPS - 1) as j:
                    u = Units(base, e * E_STEPS + j, E_UNITS)
                    e_load_in(u, 0, e, j + 1)
                    e_load_out(u, E_IN, e * E_STEPS + j)
                e_load_out(Units(base + (MOE_STEPS - 1) * E_UNITS), 0, MOE_STEPS - 1)

            def store(p):
                for b in range(TB):
                    sp.wait_ge(out_ready, TB * p + b + 1)
                    sp.dma_start(out_v[:, b, :], OUT[:, b, :]).then_inc(out_stored, 16)
                sp.wait_ge(out_stored, 32 * (p + 1))

            moe_loads(0)
            store(0)
            with overflow(sp):
                moe_loads(1)
                store(1)
                sp.nop()

        @block.gpsimd
        def _(pool):
            def ada_load(chunk, w, col, first=False, turn=0):
                for k in range(KT):
                    n = chunk * KT + k
                    if not (first and k < ADA_SLOTS):
                        pool.wait_ge(ada_used, turn * KT + (n - ADA_SLOTS + 1) if chunk_dynamic(turn)
                                     else n - ADA_SLOTS + 1)
                    pool.dma_start(ADA[:, k % ADA_SLOTS, :], w.rearrange("(p k) n -> k p n", p=P)[k][:, bass.ds(col, D)]
                                   ).then_inc(ada_landed[k % ADA_SLOTS], 16)

            ada_load(0, t["ada_w"][0], 0, first=True)
            for rows in (MOD[:, 2:5, :], MOD[:, 6, :]):
                pool.memset(rows, 0.0).then_inc(mod_cleared, 1)
            pool.wait_ge(mod_cleared, 2)
            pool.dma_start(MOD[0:1, 2:5, :], t["ada_b"][0:1, 2 * D:5 * D].rearrange("o (c n) -> o c n", c=3)
                           ).then_inc(modb_landed, 16)
            pool.dma_start(MOD[0:1, 6, :], t["ada_b"][0:1, 5 * D:6 * D]).then_inc(modb_landed, 16)
            for c in range(1, ADA_EARLY):
                ada_load(c, t["ada_w"][0], c * D)

            for j in range(TOEP_SLOTS):
                pool.wait_ge(toep_dram[j], 16 * (NBIAS // TOEP_SLOTS + (j < NBIAS % TOEP_SLOTS)))
            pool.wait_ge(ada_used, ADA_EARLY * KT)
            bias_src = bass.AP(TOEP, P - 1, [[SPAN - 1, P], [P * SPAN, NBIAS], [1, 2 * P]])
            pool.dma_start(BIAS, bias_src).then_inc(bias_landed, 16)
            pool.wait_ge(bias_landed, 16)
            pool.memset(BIAS[0:64, :, 192:256], NEG).then_inc(bias_masked, 1)

            pool.wait_ge(attn["A"]["pt_psum"], TB * HEADS)
            pool.dma_start(GB, t["norm_ffn"][0:1, :].partition_broadcast(P)).then_inc(gain_landed, 16)

            pool.wait_ge(h_ready, 2 * TB)
            for rows in (MOD[:, 0:2, :], MOD[:, 5, :], MOD[:, 7:9, :]):
                pool.memset(rows, 0.0).then_inc(mod_cleared, 1)
            pool.wait_ge(h_ready, 3 * TB)
            pool.memset(MOD[:, 2:5, :], 0.0).then_inc(mod_cleared, 1)
            pool.wait_ge(mod_cleared, 6)
            pool.dma_start(MOD[0:1, 0:6, :], t["ada_b"][1:2, :].rearrange("o (c n) -> o c n", c=6)
                           ).then_inc(modb_landed, 16)
            pool.dma_start(MOD[0:1, 7:9, :], t["kv_ada_b"].rearrange("(o c n) -> o c n", o=1, c=2)
                           ).then_inc(modb_landed, 16)
            pool.dma_start(GB, t["kv_norm"].rearrange("(o n) -> o n", o=1).partition_broadcast(P)
                           ).then_inc(gain_landed, 16)
            with pool.Fori(0, 6) as c:
                ada_load(ADA_EARLY, t["ada_w"][1], c * D, turn=c)
            for c in range(2):
                ada_load(ADA_EARLY + 6 + c, t["kv_ada_w"], c * D)
            ada_load(ADA_CHUNKS - 1, t["ada_w"][0], 5 * D)

            pool.wait_ge(ada_used, ADA_CHUNKS * KT)
            pool.dma_start(BIAS, bias_src).then_inc(bias_landed, 16)
            pool.wait_ge(gain_used, 3)
            pool.dma_start(GB, t["norm_attn"][1:2, :].partition_broadcast(P)).then_inc(gain_landed, 16)
            pool.wait_ge(bias_landed, 32)
            pool.memset(BIAS[0:64, :, 192:256], NEG).then_inc(bias_masked, 1)
            pool.memset(BIAS[0:64, :, 0:64], NEG).then_inc(bias_masked, 1)
            pool.memset(BIAS[64:128, :, 0:128], NEG).then_inc(bias_masked, 1)
            pool.wait_ge(attn["B"]["pt_psum"], TB * HEADS)
            pool.dma_start(GB, t["norm_ffn"][1:2, :].partition_broadcast(P)).then_inc(gain_landed, 16)

            def scatter_matrices(p):
                pool.wait_ge(selw_ready, TB * N_EXP * p + TB)
                if p:
                    pool.wait_ge(selt_psum, N_EXP)
                pool.tensor_copy(SELW_CUR, SELW[:, 0, :, :].rearrange("p i s -> p (i s)")).then_inc(selw_cur, 1)
                with pool.Fori(1, N_EXP) as e:
                    pool.wait_ge(selw_ready, e * TB + (TB * N_EXP * p + TB))
                    pool.wait_ge(selt_psum, e + N_EXP * p)
                    pool.tensor_copy(SELW_CUR, SELW[:, bass.ds(e, 1), :, :].rearrange("p o i s -> p (o i s)")
                                     ).then_inc(selw_cur, 1)

            scatter_matrices(0)
            with overflow(pool):
                scatter_matrices(1)
                pool.nop()

        @block.scalar
        def _(act):
            chain = Chain(act, x_squares)

            def pair(b):
                return PS[:, b:b + 2, :].rearrange("p b n -> p (b n)")

            def hi(u, *units):
                for k in units:
                    act.wait_ge(w_landed[u.raw(k)], u.landed(k))
                    if u.first + k >= SPLIT_SLOTS:
                        act.wait_ge(w_used, u.count(k - SPLIT_SLOTS) + 1)
                    nc.scalar.activation(WHI[:, u.split(k), :], WRAW[:, u.raw(k), :], ACT.Copy
                                         ).then_inc(w_hi, 1)

            def hi_ff_in(u, units, turn, s0=False):
                first_step = [Units(U_FF).raw(k) for k in range(FF_IN)]
                for k in units:
                    r = u.raw(k)
                    act.wait_ge(w_landed_b[r], 16 if s0 else turn * 16 + (32 if r in first_step else 16))
                    hi(u, k)

            def squares(src, i):
                chain(nc.scalar.activation(W4[:, :], src, ACT.Square, accum_out=nx[:, i, 0:1]))

            tables = [0]

            def load_table(func):
                n = tables[0]
                tables[0] += 1
                nc.scalar.activation(rt[:, 7, n:n + 1], ones[:, 0:1], func)

            roots = [0]

            def root(ap):
                roots[0] += 1
                act.wait_ge(var_ready, roots[0])
                nc.scalar.activation(ap, ap, ACT.Sqrt).then_inc(root_ready, 1)

            def norm_root():
                for i in range(TB):
                    squares(X[:, i, :], i)
                root(nx[:, :, 1:2])

            def mod_rows(slot, bank, halves_before):
                act.wait_ge(mod_sum, halves_before + 2)
                nc.scalar.activation(MOD[:, slot, :], pair(bank), ACT.Copy).then_inc(mod_ready, 2)

            def ht_his(use, scale=None):
                for b in range(4):
                    act.wait_ge(ht_psum, 4 * use + b + 1)
                    nc.scalar.activation(
                        HT_HI[:, 2 * b:2 * b + 2, :].rearrange("p k s -> p (k s)"), PS[:, b, :], ACT.Copy,
                        **({} if scale is None else dict(scale=scale))).then_inc(ht_hi, 1)

            def transposed(first, dst_of, col, banks, total):
                for n, bank in enumerate(banks):
                    act.wait_ge(total, first + n + 1)
                    nc.scalar.activation(dst_of(n), PS[:, bank, :], ACT.Copy, scale=gcol[:, col:col + 1]
                                         ).then_inc(qkt_ready if total is qkt_psum else kbt_ready, 1)

            def attention(a):
                sems = attn[a]

                def exps(n):
                    i, span = n // HEADS, (n // HEADS + 1) * P
                    act.wait_ge(sems["negmax"], n + 1)
                    buf, c = s_buf(a, n), sm[:, n % S_BUFS, :]
                    for m in range(2):
                        if a == "B":
                            nc.scalar.activation(c[:, 6 + m:7 + m],
                                                 sinks[:, 2 * (n % HEADS) + m:2 * (n % HEADS) + m + 1], ACT.Exp,
                                                 bias=c[:, 2 + m:3 + m])
                        nc.scalar.activation(buf[:, m, 0:span], buf[:, m, 0:span], ACT.Exp,
                                             bias=c[:, 2 + m:3 + m],
                                             accum_out=c[:, 4 + m:5 + m]).then_inc(sems["expd"], 1)

                def copy_pt(n):
                    maps = 1 if a == "A" else 2
                    span = (n // HEADS + 1) * P
                    act.wait_ge(sems["pt_psum"], n + 1)
                    if n >= 2:
                        act.wait_ge(sems["pv"], n - 1)
                    nc.scalar.activation(PT[:, n % 2, 0:maps, 0:span],
                                         PS[:, 4 + n % 2, :].rearrange("p (m k) -> p m k", m=2)[:, 0:maps, 0:span],
                                         ACT.Copy).then_inc(sems["pt_ready"], 1)

                def copy_o(n):
                    i, h = n // HEADS, n % HEADS
                    act.wait_ge(sems["pv"], n + 1)
                    nc.scalar.activation(Q[:, i, h * P:(h + 1) * P], PS[:, 6 + n % 2, 0:P], ACT.Copy
                                         ).then_inc(sems["o_ready"], 1)

                n_all = TB * HEADS
                load_table(ACT.Exp)
                exps(0)
                exps(1)
                for n in range(n_all):
                    if n + 2 < n_all:
                        exps(n + 2)
                    copy_pt(n)
                    if n:
                        copy_o(n - 1)
                load_table(ACT.Sqrt)
                copy_o(n_all - 1)

            act.dma_start(relb[:, :], t["rel_bias"]).then_inc(toep_in, 16)
            act.dma_start(onehot, t["onehot"]).then_inc(toep_in, 16)
            act.wait_ge(c_landed, 16)
            nc.scalar.activation(condT[:, :], condT[:, :], ACT.Silu).then_inc(cond_ready, 1)
            small = [
                (gcol[0:64, 0:1], t["a_q_norm"].rearrange("l d -> d l")),
                (gcol[64:128, 0:1], t["a_q_norm"].rearrange("l d -> d l")),
                (gcol[0:64, 1:2], t["a_k_norm"].rearrange("l d -> d l")),
                (gcol[64:128, 1:2], t["a_k_norm"].rearrange("l d -> d l")),
                (gcol[:, 2:3], t["a_subln"].rearrange("l d -> d l")),
                (gcol[0:64, 3:4], t["b_q_norm"].rearrange("l d -> d l")),
                (gcol[64:128, 3:4], t["b_q_norm"].rearrange("l d -> d l")),
                (gcol[0:64, 4:5], t["kv_k_norm"].rearrange("(d o) -> d o", o=1)),
                (gcol[64:128, 4:5], t["kv_k_norm"].rearrange("(d o) -> d o", o=1)),
                (lamv, t["a_lambda"].rearrange("l a d -> l (a d)").partition_broadcast(P)),
                (sinks[:, :], t["b_sinks"].partition_broadcast(P)),
                (rb[:, :], t["moe_router_b"].partition_broadcast(P)),
                (wr[:, :].rearrange("p (k e) -> p k e", k=KT),
                 t["moe_router_w"].rearrange("l (k p) e -> p (l k) e", p=P)),
            ]
            assert len(small) == SMALL
            for dst, src in small:
                with nc.allow_non_contiguous_dma(reason="short columns of gains"):
                    act.dma_start(dst, src).then_inc(small_landed, 16)
            act.dma_start(GB, t["norm_attn"][0:1, :].partition_broadcast(P)).then_inc(gain_first, 16)
            for h in range(NBIAS):
                act.wait_ge(toep_mm, h + 1)
                if h >= TOEP_SLOTS:
                    act.wait_ge(toep_dram[h % TOEP_SLOTS], 16)
                nc.scalar.activation(toep_rows(h), PS[:, 4 + h % 4, 0:SPAN], ACT.Copy).then_inc(toep_sbuf, 1)
                act.wait_ge(toep_sbuf, h + 1)
                act.dma_start(TOEP.ap()[h], toep_rows(h)).then_inc(toep_dram[h % TOEP_SLOTS], 16)
            act.wait_ge(x_landed, 16)
            act.wait_ge(sq_read, 1)
            nc.scalar.activation(neglam[:, 0:2], neglam[:, 0:2], ACT.Exp).then_inc(sq_ready, 1)
            act.wait_ge(cst_landed, 16)
            load_table(ACT.Sqrt)
            norm_root()
            ht_his(0)

            u = Units(U_QKV)

            def block_squares(banks_of, width, count, heads):
                for i in range(TB):
                    act.wait_ge(sq_read, count + i)
                    nc.scalar.activation(W4[:, 0:width], banks_of(i), ACT.Square).then_inc(sq_ready, 1)
                    root(ss[:, i, 0:heads])

            hi(u, *range(0, 14))
            act.wait_ge(w_used, U_QKV + KT)
            block_squares(lambda i: pair(4 + 2 * i), D, 1, 16)
            hi(u, *range(14, 20))
            act.wait_ge(w_used, U_QKV + 2 * KT)
            block_squares(lambda i: pair(2 * i), D, 3, 16)
            hi(u, *range(20, 24))
            act.wait_ge(w_used, U_WO)
            for i in range(TB):
                nc.scalar.activation(V[:, i, :], pair(4 + 2 * i), ACT.Copy).then_inc(v_copied, 1)
            hi(u, *range(24, 30))
            transposed(0, lambda n: Q[:, n // 2, (n % 2) * 512:(n % 2) * 512 + 512], 0, range(0, 4), qkt_psum)
            transposed(4, lambda n: K[:, n // 2, (n % 2) * 512:(n % 2) * 512 + 512], 1, range(4, 8), qkt_psum)
            attention("A")
            act.wait_ge(attn["A"]["o_ready"], TB * HEADS)
            block_squares(lambda i: Q[:, i, :], D, 5, 8)
            mod_rows(MOD0[2], 4, 4)
            mod_rows(MOD0[3], 6, 6)
            ht_his(1, scale=gcol[:, 2:3])
            hi(u, *range(30, 32))
            hi_ff_in(u, range(32, 36), 0, True)

            act.wait_ge(x_new, 2)
            norm_root()
            ht_his(2)
            load_table(ACT.Silu)

            def f_silu(u, k):
                act.wait_ge(w_used, u.count(k) + 1)
                nc.scalar.activation(FSIL, PS[:, 0:2, 0:FC], ACT.Silu).then_inc(silu_ready, 1)

            def f_at(n):
                act.wait_ge(at_psum, n)
                nc.scalar.activation(AT_HI[:, :], PS[:, 2, :], ACT.Copy).then_inc(at_hi, 1)

            def mod_half(slot, chunk, half):
                act.wait_ge(mod_sum, chunk * 2 + (2 * ADA_EARLY + 1 + half))
                row = MOD[:, bass.ds(slot, 1), half * 512:half * 512 + 512].rearrange("p o n -> p (o n)")
                nc.scalar.activation(row, PS[:, 3, :], ACT.Copy).then_inc(mod_ready, 1)

            def f_pair(it, ada, late=False):
                u = Units(first, it, RAW_SLOTS) if not isinstance(it, int) else Units(first + it * RAW_SLOTS)
                for b in range(2):
                    hi_ff_in(u, range(6 * b, 6 * b + 4), it)
                    f_at(it * 2 + (b + 1))
                    hi(u, 6 * b + 4)
                    if ada is not None:
                        mod_half(ada + b, it * 2 + b, 0)
                    elif late and b:
                        mod_half(MOD0[5], ADA_LATE, 0)
                    hi(u, 6 * b + 5)
                    f_silu(u, 6 * b + 3)
                    if ada is not None:
                        mod_half(ada + b, it * 2 + b, 1)
                    elif late and b:
                        mod_half(MOD0[5], ADA_LATE, 1)

            f_silu(Units(U_FF), FF_IN - 1)
            first = U_FF + FF_IN
            with act.Fori(0, 3) as it:
                f_pair(it, it * 2)
            f_pair(3, MODKV[0])
            f_pair(4, None, late=True)
            f_at(FF_STEPS)
            u = Units(U_KV - FF_OUT)
            hi(u, *range(0, 6))

            load_table(ACT.Sqrt)
            act.wait_ge(x_new, 4)
            norm_root()
            ht_his(3)
            act.wait_ge(w_used, U_BQ)
            for i in range(TB):
                nc.scalar.activation(KV[:, i, 256:512], PS[:, 4 + i, 256:512], ACT.Copy)
            block_squares(lambda i: PS[:, 4 + i, 0:256], 256, 7, 4)
            ht_his(4)
            u = Units(U_BQ)
            hi(u, *range(0, 8))
            transposed(0, lambda n: KBT[:, 2 * n:2 * n + 2, :].rearrange("p j k -> p (j k)"), 4,
                       range(0, 2), kbt_psum)
            act.wait_ge(w_used, U_BO)
            block_squares(lambda i: pair(4 + 2 * i), D, 9, 16)
            hi(u, *range(8, 14))
            transposed(8, lambda n: Q[:, n // 2, (n % 2) * 512:(n % 2) * 512 + 512], 3, range(0, 4), qkt_psum)
            attention("B")
            ht_his(5)
            hi(u, *range(14, 20))

            nc.scalar.activation(wr_hi[:, :], wr[:, :], ACT.Copy).then_inc(wr_hi_ready, 1)
            act.wait_ge(x_new, 6)
            norm_root()
            ht_his(6)
            hi(u, 20, 21)
            load_table(ACT.Exp)
            act.wait_ge(r_by_expert, 1)
            nc.scalar.activation(by_expert, PS[0:N_EXP, 4, 0:TB * P], ACT.Copy).then_inc(r_sbuf, 1)
            act.wait_ge(r_shift, 1)
            nc.scalar.activation(rt[:, 3, :], rt[:, 3, :], ACT.Exp).then_inc(r_exp, 1)
            load_table(ACT.Silu)

            def moe(p):
                steps0 = MOE_STEPS * p

                def selt(e):
                    act.wait_ge(selt_psum, e + (N_EXP * p + 1))
                    act.wait_ge(sc_added, e * 4 + (4 * N_EXP * p + 1))
                    nc.scalar.activation(SELT_CUR, PS[:, 7, 0:TB * P], ACT.Copy).then_inc(selt_cur, 1)

                def xt(e, last=None):
                    act.wait_ge(g_psum, e + (N_EXP * p + 1))
                    if not isinstance(e, int):
                        act.wait_ge(w_used, last)
                    nc.scalar.activation(XT_HI.rearrange("p k s -> p (k s)"), pair(5), ACT.Copy
                                         ).then_inc(xt_hi, 1)

                def silu(u, k):
                    act.wait_ge(w_used, u.count(k) + 1)
                    nc.scalar.activation(ESIL, PS[:, 0, :], ACT.Silu).then_inc(e_silu, 1)

                def at(s):
                    act.wait_ge(e_at_psum, s + (steps0 + 1))
                    nc.scalar.activation(AT_HI[:, :], PS[:, 2, :], ACT.Copy).then_inc(e_at_hi, 1)

                def step(u, s):
                    hi(u, *range(0, 7))
                    at(s - 1)
                    hi(u, *range(7, 12))
                    silu(u, 7)

                def y(e, last):
                    act.wait_ge(w_used, last)
                    nc.scalar.activation(Y, pair(3), ACT.Copy).then_inc(ey_ready, 1)

                base = U_MOE + p * MOE_STEPS * E_UNITS
                xt(0)
                hi(Units(base), *range(0 if p else 6, 8))
                base += E_IN
                silu(Units(base), -1)
                with act.Fori(0, N_EXP - 1) as e:
                    with act.Fori(0, E_STEPS - 1) as j:
                        step(Units(base, e * E_STEPS + j, E_UNITS), e * E_STEPS + j + 1)
                    u = Units(base, e * E_STEPS + (E_STEPS - 1), E_UNITS)
                    selt(e)
                    xt(e + 1, u.count(-E_OUT))
                    step(u, e * E_STEPS + E_STEPS)
                    y(e, u.count(E_UNITS))
                e = N_EXP - 1
                with act.Fori(0, E_STEPS - 1) as j:
                    step(Units(base, e * E_STEPS + j, E_UNITS), j + (e * E_STEPS + 1))
                selt(e)
                at(MOE_STEPS - 1)
                hi(Units(base + (MOE_STEPS - 1) * E_UNITS), *range(0, 4))
                y(e, base + (MOE_STEPS - 1) * E_UNITS + E_OUT)

            moe(0)
            with overflow(act):
                moe(1)
                act.nop()

        @block.vector
        def _(dve):
            chain = Chain(dve, dve_chain)
            V_ = nc.vector

            def bc(ap, n):
                return ap.unsqueeze(2).broadcast_to([ap.shape[0], ap.shape[1], n])

            def lo(u, *units):
                for k in units:
                    dve.wait_ge(w_hi, u.count(k) + 1)
                    V_.tensor_tensor(WLO[:, u.split(k), :], WRAW[:, u.raw(k), :],
                                     f32(WHI[:, u.split(k), :]), ALU.subtract).then_inc(w_lo, 1)

            def products(n0, row, ks):
                for k in ks:
                    dve.wait_ge(ada_landed[k % ADA_SLOTS], n0 * (16 // ADA_SLOTS) + 16 * (k // ADA_SLOTS + 1))
                    if k or not isinstance(n0, int) or n0:
                        dve.wait_ge(ada_used, n0 + k)
                    V_.scalar_tensor_tensor(row, ADA[:, k % ADA_SLOTS, :], condT[:, k:k + 1], row,
                                            ALU.mult, ALU.add).then_inc(ada_used, 1)

            roots = [0]

            def await_root():
                roots[0] += 1
                dve.wait_ge(root_ready, roots[0])

            def rms(squares):
                dve.wait_ge(x_squares, squares)
                V_.tensor_scalar(nx[:, :, 1:2], nx[:, :, 0:1], 1.0 / D, EPS, ALU.mult, ALU.add
                                 ).then_inc(var_ready, 1)
                await_root()
                chain(V_.reciprocal(nx[:, :, 1:2], nx[:, :, 1:2]))

            def fold(scale_slot, scale, gains):
                if gains == 1:
                    dve.wait_ge(gain_first, 16)
                else:
                    dve.wait_ge(gain_landed, 16 * (gains - 1))
                V_.scalar_tensor_tensor(MOD[:, scale_slot, :], scale, 1.0, GB,
                                        ALU.add, ALU.mult).then_inc(gain_used, 1)

            def norm(scale_slot, shift, gains):
                dve.wait_ge(gain_used, gains)
                for i in range(TB):
                    chain(V_.scalar_tensor_tensor(H[:, i, :], X[:, i, :], nx[:, i, 1:2], MOD[:, scale_slot, :],
                                                  ALU.mult, ALU.mult))
                    V_.tensor_tensor(H[:, i, :], H[:, i, :], shift, ALU.add
                                     ).then_inc(h_ready, 1)

            def ht_los(use, scale=None):
                for b in range(4):
                    dve.wait_ge(ht_hi, 4 * use + b + 1)
                    dst = HT_LO[:, 2 * b:2 * b + 2, :].rearrange("p k s -> p (k s)")
                    high = f32(HT_HI[:, 2 * b:2 * b + 2, :].rearrange("p k s -> p (k s)"))
                    if scale is None:
                        V_.tensor_tensor(dst, PS[:, b, :], high, ALU.subtract).then_inc(ht_lo, 1)
                    else:
                        V_.scalar_tensor_tensor(dst, PS[:, b, :], scale, high, ALU.mult, ALU.subtract
                                                ).then_inc(ht_lo, 1)

            def head_norm(count, heads, width, src_of, dst_of, done, squares_wide=None):
                for i in range(TB):
                    dve.wait_ge(sq_ready, count + i + 1)
                    chain(V_.tensor_reduce(ss[:, i, 0:heads],
                                           W4[:, 0:heads * width].rearrange("p (h d) -> p h d", h=heads),
                                           axis=AX, op=ALU.add))
                    V_.tensor_scalar(ss[:, i, 0:heads], ss[:, i, 0:heads], 1.0 / width, EPS,
                                     ALU.mult, ALU.add).then_inc(var_ready, 1)
                    await_root()
                    V_.reciprocal(ss[:, i, 0:heads], ss[:, i, 0:heads]).then_inc(sq_read, 1)
                    dve.wait_ge(sq_read, count + i + 1)
                    for dst in dst_of(i):
                        last = V_.tensor_tensor(dst, src_of(i), bc(ss[:, i, 0:heads], width), ALU.mult)
                        last.then_inc(done, 1)

            def attention(a):
                sems = attn[a]

                def biased(n):
                    i, h = n // HEADS, n % HEADS
                    span = (i + 1) * P
                    dve.wait_ge(sems["logits"], n + 1)
                    if n >= S_BUFS:
                        dve.wait_ge(sems["pt_psum"], n - S_BUFS + 1)
                    b, buf = 2 * (n % 2), s_buf(a, n)
                    V_.tensor_tensor(buf[:, :, 0:span], PS[:, b:b + 2, 0:span],
                                     BIAS[:, 2 * h:2 * h + 2, 2 * P - span:], ALU.add
                                     ).then_inc(sems["biased"], 1)
                    dve.wait_ge(sems["biased"], n + 1)
                    mx, nm = sm[:, n % S_BUFS, 0:2], sm[:, n % S_BUFS, 2:4]
                    chain(V_.tensor_reduce(mx, buf[:, :, 0:span], axis=AX, op=ALU.max))
                    if a == "B":
                        chain(V_.tensor_tensor(mx, mx, sinks[:, 2 * h:2 * h + 2], ALU.max))
                    V_.tensor_scalar(nm, mx, -1.0, None, ALU.mult).then_inc(sems["negmax"], 1)

                def probs(n):
                    span = (n // HEADS + 1) * P
                    dve.wait_ge(sems["expd"], 2 * n + 2)
                    total, r = sm[:, n % S_BUFS, 4:6], sm[:, n % S_BUFS, 8:10]
                    buf = s_buf(a, n)
                    s0, s1 = buf[:, 0, 0:span], buf[:, 1, 0:span]
                    if a == "A":
                        chain(V_.reciprocal(r, total))
                        chain(V_.tensor_tensor(r[:, 1:2], r[:, 1:2], neglam[:, 2:3], ALU.mult))
                        chain(V_.tensor_scalar(s0, s0, r[:, 0:1], None, ALU.mult))
                        V_.scalar_tensor_tensor(s0, s1, r[:, 1:2], s0, ALU.mult, ALU.add
                                                ).then_inc(sems["probs"], 1)
                    else:
                        chain(V_.tensor_tensor(r, total, sm[:, n % S_BUFS, 6:8], ALU.add))
                        chain(V_.reciprocal(r, r))
                        V_.tensor_tensor(buf[:, :, 0:span], buf[:, :, 0:span], bc(r, span), ALU.mult
                                         ).then_inc(sems["probs"], 1)

                n_all = TB * HEADS
                biased(0)
                biased(1)
                for n in range(n_all):
                    if n + 2 < n_all:
                        biased(n + 2)
                    probs(n)

            def residual(banks_of, gate_slot, tmp_of):
                for i in range(TB):
                    chain(V_.tensor_tensor(tmp_of(i), banks_of(i), MOD[:, gate_slot, :], ALU.mult))
                    V_.tensor_tensor(X[:, i, :], X[:, i, :], tmp_of(i), ALU.add).then_inc(x_new, 1)

            def pair(b):
                return PS[:, b:b + 2, :].rearrange("p b n -> p (b n)")

            V_.memset(MOD[:, 0:2, :], 0.0).then_inc(mod_clear, 1)
            dve.wait_ge(mod_clear, 1)
            dve.wait_ge(modb_first, 16)
            dve.wait_ge(cond_ready, 1)
            products(0, MOD[:, MOD0[0], :], range(KT))

            dve.wait_ge(small_landed, 16 * SMALL)
            lv = lamv.rearrange("p (a b d) -> p a b d", a=2, b=2)
            chain(V_.tensor_tensor(lv[:, :, 0, :], lv[:, :, 0, :], lv[:, :, 1, :], ALU.mult))
            V_.tensor_reduce(neglam[:, 0:2], lv[:, :, 0, :], axis=AX, op=ALU.add).then_inc(sq_read, 1)
            products(KT, MOD[:, MOD0[1], :], range(0, 4))
            dve.wait_ge(sq_ready, 1)
            chain(V_.tensor_tensor(neglam[:, 2:3], neglam[:, 1:2], neglam[:, 0:1], ALU.subtract))
            chain(V_.tensor_scalar(neglam[:, 2:3], neglam[:, 2:3], -LAM_INIT, None, ALU.add))
            chain(V_.tensor_scalar(gcol[:, 0:1], gcol[:, 0:1], 64 ** -0.5, None, ALU.mult))
            chain(V_.tensor_scalar(gcol[:, 3:4], gcol[:, 3:4], 64 ** -0.5, None, ALU.mult))
            chain(V_.tensor_scalar(gcol[:, 2:3], gcol[:, 2:3], 1.0 - LAM_INIT, None, ALU.mult))
            products(KT, MOD[:, MOD0[1], :], range(4, 6))
            rms(2)
            products(KT, MOD[:, MOD0[1], :], range(6, 8))
            dve.wait_ge(mod_sum, 4)
            fold(MOD0[1], pair(6), 1)
            norm(MOD0[1], pair(4), 1)
            ht_los(0)

            u = Units(U_QKV)
            dve.wait_ge(modb_landed, 32)
            rest = iter([(c, k) for c in range(2, ADA_EARLY) for k in range(KT)])

            def lo_and_products(k, n):
                lo(u, k)
                for _ in range(n):
                    c, kt = next(rest)
                    products(c * KT, MOD[:, MOD0[c], :], (kt,))

            for k in range(0, 14):
                lo_and_products(k, 0 if k < 4 else 1)
            for j in range(TOEP_SLOTS):
                dve.wait_ge(toep_dram[j], 16 * (NBIAS // TOEP_SLOTS + (j < NBIAS % TOEP_SLOTS)))

            def heads_of(ap, h):
                return ap.rearrange("p (h d) -> p h d", h=h)

            head_norm(1, 16, 64, lambda i: heads_of(pair(4 + 2 * i), 16),
                      lambda i: [heads_of(Q[:, i, :], 16)], qk_norm)
            for k in range(14, 20):
                lo_and_products(k, 1)
            head_norm(3, 16, 64, lambda i: heads_of(pair(2 * i), 16),
                      lambda i: [heads_of(K[:, i, :], 16)], qk_norm)
            for k in range(20, 24):
                lo_and_products(k, 2)
            assert next(rest, None) is None
            lo(u, *range(24, 30))
            dve.wait_ge(bias_landed, 16)
            dve.wait_ge(bias_masked, 1)
            attention("A")
            dve.wait_ge(attn["A"]["o_ready"], TB * HEADS)
            head_norm(5, 8, P, lambda i: heads_of(Q[:, i, :], 8), lambda i: [heads_of(Q[:, i, :], 8)], h_ready)
            ht_los(1, scale=gcol[:, 2:3])
            lo(u, *range(30, 36))
            dve.wait_ge(w_used, U_FF)
            dve.wait_ge(mod_ready, 4)
            residual(lambda i: pair(4 + 2 * i), MOD0[2], lambda i: H[:, i, :])
            dve.wait_ge(mod_sum, 10)
            fold(MOD0[4], pair(0), 2)
            rms(4)
            norm(MOD0[4], MOD[:, MOD0[3], :], 2)
            ht_los(2)

            def f_act(n):
                dve.wait_ge(silu_ready, n)
                V_.tensor_tensor(FACT, FSIL, PS[:, 0:2, FC:2 * FC], ALU.mult).then_inc(act_ready, 1)

            def f_at(n):
                dve.wait_ge(at_hi, n)
                V_.tensor_tensor(AT_LO[:, :], PS[:, 2, :], f32(AT_HI[:, :]), ALU.subtract).then_inc(at_ready, 1)

            f_act(1)
            dve.wait_ge(modb_landed, 64)
            first = U_FF + FF_IN

            def late_products(j, ks):
                slot = (MOD1 + MODKV + (MOD0[5],))[j] if isinstance(j, int) else j
                products((j + ADA_EARLY) * KT, MOD[:, bass.ds(slot, 1), :].rearrange("p o n -> p (o n)"), ks)

            WITH_IN = ((2,), (3, 4), (5,), (6, 7))

            def f_pair(it):
                u = Units(first, it, RAW_SLOTS) if not isinstance(it, int) else Units(first + it * RAW_SLOTS)
                for b in range(2):
                    for k in range(4):
                        lo(u, 6 * b + k)
                        late_products(it * 2 + b, WITH_IN[k])
                    f_at(it * 2 + (b + 1))
                    for k in range(2):
                        lo(u, 6 * b + 4 + k)
                        late_products(it * 2 + (b + 1), (k,))
                    f_act(it * 2 + (b + 2))

            late_products(0, (0, 1))
            with dve.Fori(0, 2) as it:
                f_pair(it)
            f_pair(2)
            f_pair(3)
            u = Units(first + 4 * RAW_SLOTS)
            for b in range(2):
                for k in range(4):
                    lo(u, 6 * b + k)
                    if k < 3:
                        late_products(ADA_LATE, (3 * b + k + 2,))
                f_at(4 * 2 + b + 1)
                lo(u, 6 * b + 4, 6 * b + 5)
                f_act(4 * 2 + b + 2)
            f_at(FF_STEPS)
            u = Units(U_KV - FF_OUT)
            lo(u, *range(0, 6))
            dve.wait_ge(w_used, U_KV)
            dve.wait_ge(mod_ready, 4 + 2 * (ADA_LATE + 1))
            residual(lambda i: pair(4 + 2 * i), MOD0[5], lambda i: H[:, i, :])
            fold(MODKV[1], MOD[:, MODKV[1], :], 3)
            rms(6)
            norm(MODKV[1], MOD[:, MODKV[0], :], 3)
            ht_los(3)
            fold(MOD1[1], MOD[:, MOD1[1], :], 4)
            dve.wait_ge(ht_psum, 16)
            norm(MOD1[1], MOD[:, MOD1[0], :], 4)
            head_norm(7, 4, 64, lambda i: heads_of(PS[:, 4 + i, 0:256], 4),
                      lambda i: [KDUP[:, i, :, c, :] for c in range(2)], kdup_ready)
            ht_los(4)
            u = Units(U_BQ)
            lo(u, *range(0, 8))
            head_norm(9, 16, 64, lambda i: heads_of(pair(4 + 2 * i), 16),
                      lambda i: [heads_of(Q[:, i, :], 16)], qk_norm)
            lo(u, *range(8, 14))
            dve.wait_ge(bias_masked, 4)
            attention("B")
            ht_los(5)
            lo(u, *range(14, 20))
            dve.wait_ge(wr_hi_ready, 1)
            V_.tensor_tensor(wr_lo[:, :], wr[:, :], f32(wr_hi[:, :]), ALU.subtract).then_inc(wr_ready, 1)
            dve.wait_ge(w_used, U_MOE)
            residual(lambda i: pair(4 + 2 * i), MOD1[2], lambda i: H[:, i, :])
            fold(MOD1[4], MOD[:, MOD1[4], :], 5)
            rms(8)
            norm(MOD1[4], MOD[:, MOD1[3], :], 5)
            ht_los(6)
            lo(u, 20, 21)

            def tok_e(n):
                return rt[:, n, :].rearrange("p (i e) -> p i e", i=TB)

            logits, rank, mask, ex, wt, pos = (tok_e(n) for n in range(6))
            small = rt[:, 6, :]
            V_.memset(XACC, 0.0).then_inc(sc_added, 1)
            dve.wait_ge(r_logits, 1)
            chain(V_.tensor_tensor(logits, PS[:, 5, 0:16].rearrange("p (i e) -> p i e", i=TB),
                                   rb[:, :].unsqueeze(1).broadcast_to([P, TB, N_EXP]), ALU.add))
            shape4 = [P, TB, N_EXP, N_EXP]
            above = W4[:, 0:128].rearrange("p (i e f) -> p i e f", i=TB, e=N_EXP)
            equal = W4[:, 128:256].rearrange("p (i e f) -> p i e f", i=TB, e=N_EXP)
            other, own = logits.unsqueeze(2).broadcast_to(shape4), logits.unsqueeze(3).broadcast_to(shape4)
            lower = CST[:, CST_LOWER:].rearrange("p (e f) -> p e f", e=N_EXP).unsqueeze(1).broadcast_to(shape4)
            chain(V_.tensor_tensor(above, other, own, ALU.is_gt))
            chain(V_.tensor_tensor(equal, other, own, ALU.is_equal))
            chain(V_.tensor_tensor(equal, equal, lower, ALU.mult))
            chain(V_.tensor_tensor(above, above, equal, ALU.add))
            chain(V_.tensor_reduce(rank, above, axis=AX, op=ALU.add))
            V_.tensor_scalar(mask, rank, 1.5, None, ALU.is_lt).then_inc(mask_ready, 1)
            chain(V_.tensor_reduce(small[:, 0:2], logits, axis=AX, op=ALU.max))
            V_.tensor_tensor(ex, logits, bc(small[:, 0:2], N_EXP), ALU.subtract).then_inc(r_shift, 1)
            dve.wait_ge(r_exp, 1)
            dve.wait_ge(mask_ready, 1)
            chain(V_.tensor_tensor(ex, ex, mask, ALU.mult))
            chain(V_.tensor_reduce(small[:, 2:4], ex, axis=AX, op=ALU.add))
            chain(V_.reciprocal(small[:, 4:6], small[:, 2:4]))
            chain(V_.tensor_tensor(wt, ex, bc(small[:, 4:6], N_EXP), ALU.mult))
            dve.wait_ge(pos_psum, 1)
            chain(V_.tensor_copy(rt[:, 5, :], PS[:, 6, 0:16]))
            chain(V_.tensor_reduce(small[0:1, 6:7], PS[0:1, 6, 16:24], axis=AX, op=ALU.max))
            V_.tensor_scalar(flag[:, :], small[0:1, 6:7], float(P), None, ALU.is_gt).then_inc(flag_ready, 1)

            def moe(p):
                steps0 = MOE_STEPS * p
                if p:
                    chain(V_.tensor_scalar(rt[:, 5, :], rt[:, 5, :], -float(P), None, ALU.add))
                for e in range(N_EXP):
                    for i in range(TB):
                        V_.tensor_scalar(SEL[:, e, i, :], iota, pos[:, i, e:e + 1], mask[:, i, e:e + 1],
                                         ALU.is_equal, ALU.mult).then_inc(sel_ready, 1)

                def selw(*experts):
                    for e in experts:
                        for i in range(TB):
                            V_.tensor_scalar(SELW[:, e, i, :], iota, pos[:, i, e:e + 1], wt[:, i, e:e + 1],
                                             ALU.is_equal, ALU.mult).then_inc(selw_ready, 1)

                def xt(e):
                    dve.wait_ge(xt_hi, e + (N_EXP * p + 1))
                    V_.tensor_tensor(XT_LO.rearrange("p k s -> p (k s)"), pair(5),
                                     f32(XT_HI.rearrange("p k s -> p (k s)")), ALU.subtract).then_inc(xt_ready, 1)

                def act(s):
                    dve.wait_ge(e_silu, s + (steps0 + 1))
                    V_.tensor_tensor(EACT, ESIL, PS[:, 1, :], ALU.mult).then_inc(e_act, 1)

                def at_lo(s):
                    dve.wait_ge(e_at_hi, s + (steps0 + 1))
                    V_.tensor_tensor(AT_LO[:, :], PS[:, 2, :], f32(AT_HI[:, :]), ALU.subtract).then_inc(e_at, 1)

                def step(u, s):
                    lo(u, *range(0, 7))
                    at_lo(s - 1)
                    lo(u, *range(7, 12))
                    act(s)

                def scattered(e):
                    for n in range(4):
                        i, half = n // 2, n % 2
                        dve.wait_ge(sc_psum, e * 4 + (4 * N_EXP * p + n + 1))
                        dve.wait_ge(sc_added, e * 4 + (4 * N_EXP * p + n + 1))
                        row = XACC[:, i, half * 512:half * 512 + 512]
                        V_.tensor_tensor(row, row, PS[:, (7, 3, 4, 7)[n], :], ALU.add).then_inc(sc_added, 1)

                base = U_MOE + p * MOE_STEPS * E_UNITS
                xt(0)
                if p:
                    dve.wait_ge(out_stored, 32)
                selw(0, 1)
                lo(Units(base), *range(0 if p else 6, 7))
                selw(2, 3)
                lo(Units(base), 7)
                selw(4, 5)
                base += E_IN
                act(0)
                selw(6, 7)
                with dve.Fori(0, N_EXP - 1) as e:
                    with dve.Fori(0, E_STEPS - 1) as j:
                        step(Units(base, e * E_STEPS + j, E_UNITS), e * E_STEPS + j + 1)
                    xt(e + 1)
                    step(Units(base, e * E_STEPS + (E_STEPS - 1), E_UNITS), e * E_STEPS + E_STEPS)
                    scattered(e)
                e = N_EXP - 1
                with dve.Fori(0, E_STEPS - 1) as j:
                    step(Units(base, e * E_STEPS + j, E_UNITS), j + (e * E_STEPS + 1))
                at_lo(MOE_STEPS - 1)
                lo(Units(base + (MOE_STEPS - 1) * E_UNITS), *range(0, 4))
                scattered(e)
                dve.wait_ge(sc_added, 4 * N_EXP * (p + 1) + 1)
                if p:
                    dve.wait_ge(out_stored, 32)
                for i in range(TB):
                    chain(V_.tensor_tensor(OUT[:, i, :], XACC[:, i, :], MOD[:, MOD1[5], :], ALU.mult))
                    V_.tensor_tensor(OUT[:, i, :], OUT[:, i, :], X[:, i, :], ALU.add).then_inc(out_ready, 1)

            moe(0)
            with overflow(dve):
                moe(1)
                dve.nop()

        @block.tensor
        def _(pe):
            def mm(out, a, b, start=True, stop=True):
                return nc.tensor.matmul(out, a, b, start=start, stop=stop)

            def split_mm(out, a_hi, a_lo, w_hi_ap, w_lo_ap, start, stop):
                mm(out, a_hi, w_hi_ap, start, False)
                mm(out, a_hi, w_lo_ap, False, False)
                return mm(out, a_lo, w_hi_ap, False, stop)

            def split_ready(u, k):
                pe.wait_ge(w_lo, u.count(k) + 1)

            def project(u, k0, bank):
                for k in range(KT):
                    split_ready(u, k0 + k)
                    s = u.split(k0 + k)
                    for i in range(TB):
                        rows = slice(i * P, i * P + P)
                        for half in range(2):
                            cols = slice(half * 512, half * 512 + 512)
                            last = split_mm(PS[:, bank + 2 * i + half, :], HT_HI[:, k, rows], HT_LO[:, k, rows],
                                            WHI[:, s, cols], WLO[:, s, cols], k == 0, k == KT - 1)
                    last.then_inc(w_used, 1)

            def ht_transposes(src, ready, counts):
                for i in range(TB):
                    pe.wait_ge(ready, counts[i])
                    for k in range(KT):
                        at = (k % 2) * 256 + i * P
                        last = nc.tensor.transpose(PS[:, k // 2, at:at + P], src[:, i, k * P:(k + 1) * P], ident)
                        if i == TB - 1 and k % 2:
                            last.then_inc(ht_psum, 1)

            def block_transposes(src, first_bank, total):
                for n in range(4):
                    i, hb = n // 2, n % 2
                    for h in range(4):
                        c = hb * 512 + h * P
                        last = nc.tensor.transpose(PS[:, first_bank + n, h * P:(h + 1) * P],
                                                   src[:, i, c:c + P], ident)
                    last.then_inc(total, 1)

            def attention(a):
                sems = attn[a]

                def logits(n):
                    i, h = n // HEADS, n % HEADS
                    if n >= 2:
                        pe.wait_ge(sems["biased"], n - 1)
                    for m in range(2):
                        rows = slice(m * 64, m * 64 + 64)
                        if a == "A":
                            keys = K[rows, 0:i + 1, h * P:(h + 1) * P]
                        else:
                            keys = KBT[rows, h // 2, 0:(i + 1) * P]
                        last = mm(PS[:, 2 * (n % 2) + m, 0:(i + 1) * P], Q[rows, i, h * P:(h + 1) * P], keys)
                    last.then_inc(sems["logits"], 1)

                def transposes(n):
                    i = n // HEADS
                    pe.wait_ge(sems["probs"], n + 1)
                    if n >= 2:
                        pe.wait_ge(sems["pt_ready"], n - 1)
                    for m in range(1 if a == "A" else 2):
                        for kt in range(i + 1):
                            at = m * 256 + kt * P
                            last = nc.tensor.transpose(PS[:, 4 + n % 2, at:at + P],
                                                       s_buf(a, n)[:, m, kt * P:(kt + 1) * P], ident)
                    last.then_inc(sems["pt_psum"], 1)

                def products(n):
                    i, h = n // HEADS, n % HEADS
                    pe.wait_ge(sems["pt_ready"], n + 1)
                    if n >= 2:
                        pe.wait_ge(sems["o_ready"], n - 1)
                    bank = 6 + n % 2
                    if a == "A":
                        for kt in range(i + 1):
                            last = mm(PS[:, bank, 0:P], PT[:, n % 2, 0, kt * P:(kt + 1) * P],
                                      V[:, kt, h * P:(h + 1) * P], kt == 0, kt == i)
                    else:
                        j = h // 2
                        for m in range(2):
                            for kt in range(i + 1):
                                last = mm(PS[:, bank, m * 64:(m + 1) * 64], PT[:, n % 2, m, kt * P:(kt + 1) * P],
                                          KV[:, kt, 256 + j * 64:256 + (j + 1) * 64], kt == 0, kt == i)
                    last.then_inc(sems["pv"], 1)

                n_all = TB * HEADS
                logits(0)
                logits(1)
                logits(2)
                for n in range(n_all):
                    if n + 3 < n_all:
                        logits(n + 3)
                    transposes(n)
                    if n:
                        products(n - 1)
                products(n_all - 1)

            pe.wait_ge(toep_in, 32)
            for h in range(NBIAS):
                if h >= 4:
                    pe.wait_ge(toep_sbuf, h - 3)
                mm(PS[:, 4 + h % 4, 0:SPAN], relb[:, h:h + 1].broadcast_to([32, P]), onehot).then_inc(toep_mm, 1)
            pe.wait_ge(cst_landed, 16)

            def mod_sums(c, bank):
                pe.wait_ge(ada_used, KT * (c + 1))
                for half in range(2):
                    mm(PS[:, bank + half, :], ones, MOD[:, MOD0[c], half * 512:half * 512 + 512]
                       ).then_inc(mod_sum, 1)

            pe.wait_ge(toep_sbuf, NBIAS)
            mod_sums(0, 4)
            mod_sums(1, 6)

            u = Units(U_QKV)
            ht_transposes(H, h_ready, (1, 2))
            pe.wait_ge(ht_lo, 4)
            project(u, 0, 4)
            project(u, KT, 0)
            pe.wait_ge(qk_norm, 2)
            project(u, 2 * KT, 4)
            pe.wait_ge(qk_norm, 4)
            block_transposes(Q, 0, qkt_psum)
            pe.wait_ge(v_copied, 2)
            block_transposes(K, 4, qkt_psum)
            pe.wait_ge(qkt_ready, 8)
            attention("A")
            mod_sums(2, 4)
            pe.wait_ge(attn["A"]["o_ready"], TB * HEADS)
            mod_sums(3, 6)
            ht_transposes(Q, h_ready, (3, 4))
            pe.wait_ge(ht_lo, 8)
            pe.wait_ge(mod_ready, 4)
            project(Units(U_WO), 0, 4)
            mod_sums(4, 0)
            ht_transposes(H, h_ready, (5, 6))
            pe.wait_ge(ht_lo, 12)

            def f_in(u, k0, ks, first, last):
                for k in ks:
                    split_ready(u, k0 + k)
                    s = u.split(k0 + k)
                    for kt in range(2):
                        cols, kk = slice(kt * 512, kt * 512 + 512), 2 * k + kt
                        for i in range(TB):
                            rows = slice(i * P, i * P + P)
                            x = split_mm(PS[:, i, :], HT_HI[:, kk, rows], HT_LO[:, kk, rows], WHI[:, s, cols],
                                         WLO[:, s, cols], kk == 0, kk == KT - 1)
                    x.then_inc(w_used, 1)

            def f_transposes(n):
                pe.wait_ge(act_ready, n)
                for c in range(2):
                    for i in range(TB):
                        last = nc.tensor.transpose(PS[:, 2, c * 256 + i * P:c * 256 + i * P + P],
                                                   FACT[:, i, c * P:(c + 1) * P], ident)
                last.then_inc(at_psum, 1)

            def f_out(u, k0, c, start, stop):
                split_ready(u, k0)
                s = u.split(k0)
                for i in range(TB):
                    rows = slice(c * 256 + i * P, c * 256 + i * P + P)
                    for half in range(2):
                        cols = slice(half * 512, half * 512 + 512)
                        last = split_mm(PS[:, 4 + 2 * i + half, :], AT_HI[:, rows], AT_LO[:, rows],
                                        WHI[:, s, cols], WLO[:, s, cols], start, stop)
                last.then_inc(w_used, 1)
                return last

            def mod_half(slot, chunk, half):
                if half == 0:
                    pe.wait_ge(ada_used, (chunk + (ADA_EARLY + 1)) * KT)
                pe.wait_ge(mod_ready, chunk * 2 + (4 + half))
                row = MOD[:, bass.ds(slot, 1), half * 512:half * 512 + 512].rearrange("p o n -> p (o n)")
                mm(PS[:, 3, :], ones, row).then_inc(mod_sum, 1)

            u = Units(U_FF)
            f_in(u, 0, range(4), True, False)
            first = U_FF + FF_IN

            def f_pair(it, ada, clears, late=False):
                u = Units(first, it, RAW_SLOTS) if not isinstance(it, int) else Units(first + it * RAW_SLOTS)
                for b in range(2):
                    pe.wait_ge(act_ready, it * 2 + (b + 1))
                    f_in(u, 6 * b, (0, 1), True, False)
                    f_transposes(it * 2 + (b + 1))
                    f_in(u, 6 * b, (2, 3), True, False)
                    if ada is not None:
                        mod_half(ada + b, it * 2 + b, 0)
                    elif late and b:
                        mod_half(MOD0[5], ADA_LATE, 0)
                    pe.wait_ge(at_ready, it * 2 + (b + 1))
                    f_out(u, 6 * b + 4, 0, clears and b == 0, False)
                    if ada is not None:
                        mod_half(ada + b, it * 2 + b, 1)
                    elif late and b:
                        mod_half(MOD0[5], ADA_LATE, 1)
                    f_out(u, 6 * b + 5, 1, False, False)

            f_pair(0, 0, True)
            with pe.Fori(1, 3) as it:
                f_pair(it, it * 2, False)
            f_pair(3, MODKV[0], False)
            f_pair(4, None, False, late=True)
            u = Units(U_KV - FF_OUT)
            f_transposes(FF_STEPS)
            pe.wait_ge(at_ready, FF_STEPS)
            f_out(u, 0, 0, False, False)
            f_out(u, 1, 1, False, True)

            ht_transposes(H, h_ready, (7, 8))
            pe.wait_ge(ht_lo, 16)
            u = Units(U_KV)
            for k in range(KT // 2):
                split_ready(u, k)
                s = u.split(k)
                for kt in range(2):
                    cols, kk = slice(kt * 512, kt * 512 + 512), 2 * k + kt
                    for i in range(TB):
                        rows = slice(i * P, i * P + P)
                        last = split_mm(PS[:, 4 + i, :], HT_HI[:, kk, rows], HT_LO[:, kk, rows], WHI[:, s, cols],
                                        WLO[:, s, cols], kk == 0, kk == KT - 1)
                last.then_inc(w_used, 1)
            ht_transposes(H, h_ready, (9, 10))
            pe.wait_ge(ht_lo, 20)
            pe.wait_ge(kdup_ready, 4)
            project(Units(U_BQ), 0, 4)
            for b in range(2):
                for j in (2 * b, 2 * b + 1):
                    for i in range(TB):
                        at = (j % 2) * 256 + i * P
                        last = nc.tensor.transpose(PS[:, b, at:at + P],
                                                   KDUP[:, i, j, :, :].rearrange("p c d -> p (c d)"), ident)
                last.then_inc(kbt_psum, 1)
            pe.wait_ge(qk_norm, 6)
            pe.wait_ge(kbt_ready, 2)
            block_transposes(Q, 0, qkt_psum)
            pe.wait_ge(qkt_ready, 12)
            attention("B")
            ht_transposes(Q, attn["B"]["o_ready"], (HEADS, TB * HEADS))
            pe.wait_ge(ht_lo, 24)
            project(Units(U_BO), 0, 4)
            ht_transposes(H, h_ready, (11, 12))
            pe.wait_ge(ht_lo, 28)

            pe.wait_ge(wr_ready, 1)
            for k in range(KT):
                e = slice(k * N_EXP, (k + 1) * N_EXP)
                last = split_mm(PS[0:N_EXP, 4, 0:TB * P], wr_hi[:, e], wr_lo[:, e], HT_HI[:, k, :], HT_LO[:, k, :],
                                k == 0, k == KT - 1)
            last.then_inc(r_by_expert, 1)
            pe.wait_ge(r_sbuf, 1)
            for i in range(TB):
                last = nc.tensor.transpose(PS[:, 5, i * N_EXP:(i + 1) * N_EXP], by_expert[:, i * P:(i + 1) * P],
                                           ident[0:N_EXP, 0:N_EXP])
            last.then_inc(r_logits, 1)
            pe.wait_ge(mask_ready, 1)
            m0, m1 = rt[:, 2, 0:N_EXP], rt[:, 2, N_EXP:2 * N_EXP]
            mm(PS[:, 6, 0:8], tri, m0)
            mm(PS[:, 6, 8:16], ones, m0, True, False)
            mm(PS[:, 6, 8:16], tri, m1, False, True)
            mm(PS[:, 6, 16:24], ones, m0, True, False)
            mm(PS[:, 6, 16:24], ones, m1, False, True).then_inc(pos_psum, 1)

            def moe(p):
                steps0 = MOE_STEPS * p
                if p:
                    pe.wait_ge(sc_added, 4 * N_EXP + 1)
                pe.wait_ge(sel_ready, TB * N_EXP * p + TB)

                def gather(e):
                    for k in range(KT):
                        out = PS[:, 5 + k // 4, (k % 4) * P:(k % 4) * P + P]
                        for i in range(TB):
                            sel = SEL[:, e, i, :] if isinstance(e, int) else SEL[
                                :, bass.ds(e, 1), i, :].rearrange("p o s -> p (o s)")
                            last = mm(out, H[:, i, k * P:(k + 1) * P], sel, i == 0, i == 1)
                    last.then_inc(g_psum, 1)

                def e_in(u, ks):
                    for k in ks:
                        split_ready(u, k)
                        s = u.split(k)
                        start, stop = k == 0, k == KT - 1
                        gate, up = slice(0, 512), slice(512, 1024)
                        xh, xl = XT_HI[:, k, :], XT_LO[:, k, :]
                        mm(PS[:, 0, :], xh, WHI[:, s, gate], start, False)
                        mm(PS[:, 0, :], xh, WLO[:, s, gate], False, False)
                        mm(PS[:, 1, :], xh, WHI[:, s, up], start, False)
                        mm(PS[:, 1, :], xh, WLO[:, s, up], False, False)
                        mm(PS[:, 0, :], xl, WHI[:, s, gate], False, stop)
                        last = mm(PS[:, 1, :], xl, WHI[:, s, up], False, stop)
                        last.then_inc(w_used, 1)

                def e_transposes(s):
                    pe.wait_ge(e_act, s + (steps0 + 1))
                    for c in range(4):
                        last = nc.tensor.transpose(PS[:, 2, c * P:(c + 1) * P], EACT[:, c * P:(c + 1) * P], ident)
                    last.then_inc(e_at_psum, 1)

                def e_out(u, k0, s, start, stop):
                    pe.wait_ge(e_at, s + (steps0 + 1))
                    for c in range(4):
                        split_ready(u, k0 + c)
                        slot, rows = u.split(k0 + c), slice(c * P, (c + 1) * P)
                        for half in range(2):
                            cols = slice(half * 512, half * 512 + 512)
                            last = split_mm(PS[:, 3 + half, :], AT_HI[:, rows], AT_LO[:, rows],
                                            WHI[:, slot, cols], WLO[:, slot, cols],
                                            start and c == 0, stop and c == 3)
                        last.then_inc(w_used, 1)

                def step(u, s, start, stop):
                    pe.wait_ge(e_act, s + steps0)
                    e_in(u, range(0, 4))
                    e_transposes(s - 1)
                    e_in(u, range(4, 8))
                    e_out(u, 8, s - 1, start, stop)

                def scatter(e):
                    pe.wait_ge(ey_ready, e + (N_EXP * p + 1))
                    pe.wait_ge(selt_cur, e + (N_EXP * p + 1))
                    for n in range(4):
                        i, half = n // 2, n % 2
                        if n == 3:
                            pe.wait_ge(sc_added, e * 4 + (4 * N_EXP * p + 2))
                        mm(PS[:, (7, 3, 4, 7)[n], :], SELT_CUR[:, i * P:(i + 1) * P],
                           Y[:, half * 512:half * 512 + 512]).then_inc(sc_psum, 1)

                base = U_MOE + p * MOE_STEPS * E_UNITS
                gather(0)
                pe.wait_ge(xt_ready, N_EXP * p + 1)
                e_in(Units(base), range(0, 8))
                base += E_IN
                pe.wait_ge(sel_ready, TB * N_EXP * (p + 1))

                def expert(e):
                    if not (isinstance(e, int) and e == N_EXP - 1):
                        gather(e + 1)
                    turn = e * E_STEPS
                    u = Units(base, turn, E_UNITS) if not isinstance(e, int) else Units(base + turn * E_UNITS)
                    pe.wait_ge(sc_added, e * 4 + (4 * N_EXP * p + 1))
                    pe.wait_ge(selw_cur, e + (N_EXP * p + 1))
                    for i in range(TB):
                        last = nc.tensor.transpose(PS[:, 7, i * P:(i + 1) * P], SELW_CUR[:, i * P:(i + 1) * P],
                                                   ident)
                    last.then_inc(selt_psum, 1)
                    step(u, turn + 1, True, False)
                    with pe.Fori(1, E_STEPS - 1) as j:
                        step(Units(base, turn + j, E_UNITS), j + (turn + 1), False, False)

                with pe.Fori(0, N_EXP - 1) as e:
                    expert(e)
                    pe.wait_ge(xt_ready, e + (N_EXP * p + 2))
                    u = Units(base, e * E_STEPS + (E_STEPS - 1), E_UNITS)
                    step(u, e * E_STEPS + E_STEPS, False, True)
                    scatter(e)
                e = N_EXP - 1
                expert(e)
                u = Units(base + (MOE_STEPS - 1) * E_UNITS)
                e_transposes(MOE_STEPS - 1)
                e_out(u, 0, MOE_STEPS - 1, False, True)
                scatter(e)

            moe(0)
            with overflow(pe):
                moe(1)
                pe.nop()


_INS = ["x", "c", "ada_w", "ada_b", "norm_attn", "norm_ffn", "rel_bias", "a_w_qkv", "a_q_norm", "a_k_norm",
        "a_lambda", "a_subln", "a_w_o", "kv_ada_w", "kv_ada_b", "kv_norm", "kv_w", "kv_k_norm", "b_w_q",
        "b_q_norm", "b_sinks", "b_w_o", "ffn_w_in", "ffn_w_out", "moe_router_w", "moe_router_b", "moe_w_in",
        "moe_w_out"]


def t5_bucket(rel):
    nb = 16
    ret = (rel > 0).astype(np.int32) * nb
    n = np.abs(rel)
    exact = nb // 2
    large = exact + (np.log(np.maximum(n, 1) / exact) / np.log(128 / exact) * (nb - exact)).astype(np.int32)
    return ret + np.where(n < exact, n, np.minimum(large, nb - 1))


def constants():
    cst = np.zeros((P, CST_COLS), np.float32)
    r = np.arange(P)
    cst[:, CST_IDENT:CST_IDENT + P] = r[:, None] == r[None, :]
    cst[:, CST_TRI:CST_TRI + P] = r[:, None] < r[None, :]
    cst[:, CST_IOTA:CST_IOTA + P] = r[None, :]
    cst[:, CST_ONES:CST_ONES + P] = 1.0
    e = np.arange(N_EXP)
    cst[:, CST_LOWER:] = (e[None, :] < e[:, None]).astype(np.float32).reshape(1, -1)
    onehot = np.zeros((32, SPAN), np.float32)
    i = np.arange(SPAN)
    onehot[t5_bucket(i - 255), i] = 1.0
    return cst, onehot


def kernel(**inputs):
    import concourse.bacc as _bacc
    from concourse.bass_utils import run_bass_kernel_spmd as _run

    nc = _bacc.Bacc("TRN2", target_bir_lowering=False, num_devices=1)
    arrays, t = {}, {}
    data = {n: inputs[n] for n in _INS}
    data["cst"], data["onehot"] = constants()
    for name, value in data.items():
        a = np.ascontiguousarray(value)
        arrays[f"in_{name}"] = a
        t[name] = nc.dram_tensor(f"in_{name}", a.shape, mybir.dt.from_np(a.dtype), kind="ExternalInput").ap()
    t["out"] = nc.dram_tensor("out_x", inputs["x"].shape, F32, kind="ExternalOutput").ap()
    trunk(nc, t)
    r = _run(nc, [arrays], core_ids=[0])
    return r.results[0]["out_x"]
```
